# Optimizing a Trainium2 kernel written in Bass

```python
import math
import jax, jax.numpy as jnp
from jax import lax
import numpy as np

D_MODEL = 1024
BATCH = 1
SEQ = 512
DEPTH = 2

HEAD_DIM = 64
SB_HEADS = D_MODEL // HEAD_DIM
SW_Q_HEADS = D_MODEL // HEAD_DIM
SW_KV_HEADS = 4
WINDOW = 128
BLOCK = 128
PEER_HEADS = 8
PEER_KEYS = 128
PEER_N_EXPERTS = PEER_KEYS * PEER_KEYS
PEER_QDIM = 256
PEER_HALF = PEER_QDIM // 2
PEER_TOPK = 16
PEER_CHUNK = 128
RMS_EPS = 1e-6
N_SB = (DEPTH + 1) // 2
N_SW = DEPTH // 2

kernel_name = 'hybrid_stickbreak_swa_sink_peer'

def rmsnorm(x, gain):
    xf = x.astype(jnp.float32)
    y = xf * lax.rsqrt(jnp.mean(xf * xf, axis=-1, keepdims=True) + RMS_EPS)
    return (y * gain.astype(jnp.float32)).astype(x.dtype)

def alibi_slopes(n_heads):
    return jnp.asarray(2.0 ** (-8.0 * np.arange(1, n_heads + 1) / n_heads), dtype=jnp.float32)

def stick_breaking_attention(x, w_qkv, w_o):
    B, S, _ = x.shape
    qkv = x @ w_qkv
    q, k, v = jnp.split(qkv, 3, axis=-1)
    to_heads = lambda a: a.reshape(B, S, SB_HEADS, HEAD_DIM).transpose(0, 2, 1, 3)
    q, k, v = to_heads(q), to_heads(k), to_heads(v)
    scale = HEAD_DIM ** -0.5
    outs = []
    for n in range(S // BLOCK):
        t0 = n * BLOCK
        end = t0 + BLOCK
        z = jnp.einsum('bhtd,bhsd->bhts', q[:, :, t0:end], k[:, :, :end]).astype(jnp.float32) * scale
        t_pos = t0 + jnp.arange(BLOCK)[:, None]
        s_pos = jnp.arange(end)[None, :]
        causal = s_pos < t_pos
        log_fail = jnp.where(causal, jax.nn.log_sigmoid(-z), 0.0)
        suffix = lax.cumsum(log_fail, axis=3, reverse=True) - log_fail
        log_a = jax.nn.log_sigmoid(z) + suffix
        a = jnp.where(causal, jnp.exp(log_a), 0.0)
        outs.append(jnp.einsum('bhts,bhsd->bhtd', a.astype(v.dtype), v[:, :, :end]))
    o = jnp.concatenate(outs, axis=2)
    o = o.transpose(0, 2, 1, 3).reshape(B, S, SB_HEADS * HEAD_DIM)
    return o @ w_o

def sliding_window_attention(x, w_qkv, q_gain, k_gain, sinks, w_o):
    B, S, _ = x.shape
    G = SW_Q_HEADS // SW_KV_HEADS
    nb = S // BLOCK
    qkv = x @ w_qkv
    q, k, v = jnp.split(qkv, [SW_Q_HEADS * HEAD_DIM, (SW_Q_HEADS + SW_KV_HEADS) * HEAD_DIM], axis=-1)
    q = rmsnorm(q.reshape(B, S, SW_KV_HEADS, G, HEAD_DIM), q_gain)
    k = rmsnorm(k.reshape(B, S, SW_KV_HEADS, HEAD_DIM), k_gain)
    v = v.reshape(B, S, SW_KV_HEADS, HEAD_DIM)
    qb = q.reshape(B, nb, BLOCK, SW_KV_HEADS, G, HEAD_DIM)

    def band(a):
        a = jnp.pad(a, ((0, 0), (BLOCK, 0), (0, 0), (0, 0)))
        a = a.reshape(B, nb + 1, BLOCK, SW_KV_HEADS, HEAD_DIM)
        return jnp.concatenate([a[:, :-1], a[:, 1:]], axis=2)

    kb, vb = band(k), band(v)
    scores = jnp.einsum('bnikgd,bnjkd->bnkgij', qb, kb).astype(jnp.float32) * (HEAD_DIM ** -0.5)
    i = jnp.arange(BLOCK)[:, None]
    j = jnp.arange(2 * BLOCK)[None, :]
    dist = BLOCK + i - j
    blk = jnp.arange(nb)[:, None, None]
    valid = (dist >= 0) & (dist < WINDOW) & (blk * BLOCK + j - BLOCK >= 0)
    slopes = alibi_slopes(SW_Q_HEADS).reshape(SW_KV_HEADS, G)
    scores = scores - slopes[:, :, None, None] * dist.astype(jnp.float32)
    scores = jnp.where(valid[None, :, None, None], scores, -jnp.inf)
    sink = sinks.astype(jnp.float32).reshape(SW_KV_HEADS, G)
    m = jnp.maximum(jnp.max(scores, axis=-1), sink[:, :, None])
    p = jnp.exp(scores - m[..., None])
    denom = jnp.sum(p, axis=-1) + jnp.exp(sink[:, :, None] - m)
    probs = (p / denom[..., None]).astype(vb.dtype)
    o = jnp.einsum('bnkgij,bnjkd->bnikgd', probs, vb)
    o = o.reshape(B, S, SW_Q_HEADS * HEAD_DIM)
    return o @ w_o

def peer(x, w_query, sub_keys, expert_u, expert_v):
    B, S, D = x.shape
    T = B * S
    xt = x.reshape(T, D)
    q = (xt @ w_query).reshape(T, PEER_HEADS, 2, PEER_HALF)
    sc = jnp.einsum('thpc,hpnc->thpn', q, sub_keys).astype(jnp.float32)
    top_s, top_i = lax.top_k(sc, PEER_TOPK)
    cand = top_s[:, :, 0, :, None] + top_s[:, :, 1, None, :]
    cand_s, cand_i = lax.top_k(cand.reshape(T, PEER_HEADS, PEER_TOPK * PEER_TOPK), PEER_TOPK)
    i1 = jnp.take_along_axis(top_i[:, :, 0], cand_i // PEER_TOPK, axis=-1)
    i2 = jnp.take_along_axis(top_i[:, :, 1], cand_i % PEER_TOPK, axis=-1)
    expert = i1 * PEER_KEYS + i2
    gate = jax.nn.softmax(cand_s, axis=-1)

    def chunk(args):
        xc, ec, gc = args
        h = jnp.einsum('cd,chkd->chk', xc, expert_u[ec])
        coef = (gc * jax.nn.gelu(h.astype(jnp.float32))).astype(xc.dtype)
        return jnp.einsum('chk,chkd->cd', coef, expert_v[ec])

    nc = T // PEER_CHUNK
    out = lax.map(chunk, (xt.reshape(nc, PEER_CHUNK, D),
                          expert.reshape(nc, PEER_CHUNK, PEER_HEADS, PEER_TOPK),
                          gate.reshape(nc, PEER_CHUNK, PEER_HEADS, PEER_TOPK)))
    return out.reshape(B, S, D)

def setup_inputs(seed: int = 0) -> dict:
    key = jax.random.key(seed)
    ks = jax.random.split(key, 16)
    nrm = lambda k, shape, s: jax.random.normal(k, shape, jnp.float32) * s
    gain = lambda k, shape: 1.0 + 0.02 * jax.random.normal(k, shape, jnp.float32)
    d_inv = D_MODEL ** -0.5
    sw_cols = (SW_Q_HEADS + 2 * SW_KV_HEADS) * HEAD_DIM
    return {
        'x': jax.random.normal(ks[0], (BATCH, SEQ, D_MODEL), jnp.float32),
        'sb_norm': gain(ks[1], (N_SB, D_MODEL)),
        'sb_w_qkv': nrm(ks[2], (N_SB, D_MODEL, 3 * SB_HEADS * HEAD_DIM), d_inv),
        'sb_w_o': nrm(ks[3], (N_SB, SB_HEADS * HEAD_DIM, D_MODEL), d_inv),
        'sw_norm': gain(ks[4], (N_SW, D_MODEL)),
        'sw_w_qkv': nrm(ks[5], (N_SW, D_MODEL, sw_cols), d_inv),
        'sw_q_gain': gain(ks[6], (N_SW, HEAD_DIM)),
        'sw_k_gain': gain(ks[7], (N_SW, HEAD_DIM)),
        'sw_sinks': nrm(ks[8], (N_SW, SW_Q_HEADS), 0.5),
        'sw_w_o': nrm(ks[9], (N_SW, SW_Q_HEADS * HEAD_DIM, D_MODEL), d_inv),
        'ffn_norm': gain(ks[10], (DEPTH, D_MODEL)),
        'peer_w_query': nrm(ks[11], (DEPTH, D_MODEL, PEER_HEADS * PEER_QDIM), d_inv),
        'peer_sub_keys': nrm(ks[12], (DEPTH, PEER_HEADS, 2, PEER_KEYS, PEER_HALF), PEER_HALF ** -0.5),
        'peer_u': nrm(ks[13], (DEPTH, PEER_N_EXPERTS, D_MODEL), d_inv),
        'peer_v': nrm(ks[14], (DEPTH, PEER_N_EXPERTS, D_MODEL), PEER_HEADS ** -0.5),
    }

def reference(x, sb_norm, sb_w_qkv, sb_w_o, sw_norm, sw_w_qkv, sw_q_gain, sw_k_gain, sw_sinks, sw_w_o,
              ffn_norm, peer_w_query, peer_sub_keys, peer_u, peer_v):
    h = x
    for i in range(DEPTH):
        j = i // 2
        if i % 2 == 0:
            h = h + stick_breaking_attention(rmsnorm(h, sb_norm[j]), sb_w_qkv[j], sb_w_o[j])
        else:
            h = h + sliding_window_attention(rmsnorm(h, sw_norm[j]), sw_w_qkv[j], sw_q_gain[j],
                                             sw_k_gain[j], sw_sinks[j], sw_w_o[j])
        h = h + peer(rmsnorm(h, ffn_norm[i]), peer_w_query[i], peer_sub_keys[i], peer_u[i], peer_v[i])
    return h


_drawn_inputs = setup_inputs


def setup_inputs(seed=0):
    import zlib

    import numpy as np

    out = dict(_drawn_inputs(seed))
    spreads = {}
    factors = {'sw_norm': 3.661, 'sw_q_gain': 5.129, 'sw_k_gain': 5.121, 'sw_sinks': 40.936}
    for name, (base, spread) in spreads.items():
        noise = np.random.default_rng([zlib.crc32(name.encode()), seed]).standard_normal(out[name].shape)
        drawn = base * np.exp(spread * noise) if base else spread * noise
        out[name] = __import__('jax').numpy.asarray(drawn.astype(out[name].dtype))
    for name, factor in factors.items():
        out[name] = (out[name] * factor).astype(out[name].dtype)
    return out
```

```python
from contextlib import ExitStack

import concourse.bass as bass
import numpy as np
from concourse import mybir

F32 = mybir.dt.float32
BF16 = mybir.dt.bfloat16
U32 = mybir.dt.uint32
ALU = mybir.AluOpType
ACT = mybir.ActivationFunctionType
AX_X = mybir.AxisListType.X

P = 128
D = 1024
S = 512
TT = S // P
KC = D // P
BANK = 512
HALVES = D // BANK
DH = 64
SCALE = DH ** -0.5
PAIRS = D // P
KV_PAIRS = 2
GROUP = 4
SW_HEADS = 16
WIN = 2 * P
PEER_HEADS = 8
KEYS = 128
TOPK = 16
TOP8 = 8
UNITS = PEER_HEADS * TT
SLOTS = 8
CREDIT = 1
RMS_EPS = 1e-6
MASKED = -1.0e30
LOWEST = -3.0e38
HUGE = 3.0e37
GELU_C = 2.0 * (2.0 / np.pi) ** 0.5
GELU_A = 0.044715


def spread(ap, axis, shape):
    return ap.unsqueeze(axis).broadcast_to(shape)


def build(nc, x, sb_norm, sb_w_qkv, sb_w_o, sw_norm, sw_w_qkv, sw_q_gain, sw_k_gain, sw_sinks, sw_w_o,
          ffn_norm, peer_w_query, peer_sub_keys, peer_u, peer_v, out):
    x_tiles = x[0].rearrange("(t p) d -> t p d", p=P)
    out_tiles = out[0].rearrange("(t p) d -> t p d", p=P)
    gains = [sb_norm[0:1, :], ffn_norm[0:1, :], sw_norm[0:1, :], ffn_norm[1:2, :]]

    with ExitStack() as ctx:
        def sb(name, shape, dt=F32):
            return ctx.enter_context(nc.sbuf_tensor(name, shape, dt))

        def sem(name):
            return ctx.enter_context(nc.semaphore(name))

        h = sb("h", [P, TT, D])
        xn = sb("xn", [P, TT, D])
        xnT = sb("xnT", [P, KC, S])
        gain_b = sb("gain_b", [P, 2, D])
        sumsq = sb("sumsq", [P, TT])
        root = sb("root", [P, TT])
        eps = sb("eps", [P, 1])
        rstd = sb("rstd", [P, TT])
        ident = sb("ident", [P, P])
        ident_bf = sb("ident_bf", [P, P], BF16)
        later_bf = sb("later_bf", [P, P], BF16)
        slot_no = sb("slot_no", [P, TOPK])
        arena = sb("arena", [P, 2 * SLOTS * D])
        u_ring = arena[:, 0:SLOTS * D].rearrange("p (s d) -> p s d", d=D)
        v_ring = arena[:, SLOTS * D:2 * SLOTS * D].rearrange("p (s d) -> p s d", d=D)
        wo = arena[:, 0:KC * D].rearrange("p (k n) -> p k n", n=D)
        oT_all = arena[:, KC * D:KC * D + KC * S].rearrange("p (k s) -> p k s", s=S)
        bias = arena[:, KC * D + KC * S:2 * SLOTS * D].rearrange("p (h w) -> p h w", w=WIN)
        w_q = sb("w_q", [P, KC, P])
        w_k = sb("w_k", [P, KC, P])
        w_v = sb("w_v", [P, KC, P])
        qT = sb("qT", [P, S])
        kT = sb("kT", [P, S])
        v_tok = sb("v_tok", [P, TT, P])
        RING3 = 3
        work = sb("work", [P, RING3 * 4 * BANK + 8])
        fail = work[:, 0:RING3 * BANK].rearrange("p (r s) -> p r s", r=RING3)
        take = work[:, RING3 * BANK:2 * RING3 * BANK].rearrange("p (r s) -> p r s", r=RING3)
        attn = work[:, 2 * RING3 * BANK:3 * RING3 * BANK].rearrange("p (r s) -> p r s", r=RING3)
        left = work[:, 3 * RING3 * BANK:3 * RING3 * BANK + RING3 * (BANK + 1)].rearrange("p (r s) -> p r s", r=RING3)
        sc_sb = work[:, 0:2 * TT * WIN].rearrange("p (a n w) -> p a n w", a=2, n=TT)
        prob = work[:, 2 * TT * WIN:4 * TT * WIN].rearrange("p (a n w) -> p a n w", a=2, n=TT)
        head_sq = work[:, 4 * TT * WIN:4 * TT * WIN + BANK]
        head_tok = work[:, 4 * TT * WIN + BANK:4 * TT * WIN + 2 * BANK]
        attnT = sb("attnT", [P, 2, 2 * BANK])
        qk_gain = sb("qk_gain", [P, 2, DH])
        sink_b = sb("sink_b", [P, SW_HEADS])
        dist = sb("dist", [P, WIN])
        head_ss = sb("head_ss", [P, 2 * TT])
        head_root = sb("head_root", [P, 2 * TT])
        head_rstd = sb("head_rstd", [P, 2 * TT])
        top = sb("top", [P, 2, TT])
        neg_top = sb("neg_top", [P, 2, TT])
        sink_arg = sb("sink_arg", [P, 2, TT])
        sink_exp = sb("sink_exp", [P, 2, TT])
        row_sum = sb("row_sum", [P, 2, TT])
        denom = sb("denom", [P, 2, TT])
        inv_denom = sb("inv_denom", [P, 2, TT])
        w_pq = sb("w_pq", [P, KC, 2 * P])
        keys = sb("keys", [P, 2, P])
        keysT = sb("keysT", [P, 2, P])
        pqT = sb("pqT", [P, 2, S])
        scores = sb("scores", [P, TT, 2, KEYS])
        rest = sb("rest", [P, 2, KEYS])
        half_top = sb("half_top", [P, 2, TOPK])
        half_idx = sb("half_idx", [P, 2, TOPK], U32)
        half_idx_f = sb("half_idx_f", [P, 2, TOPK])
        cand = sb("cand", [P, TOPK, TOPK])
        cand_rest = sb("cand_rest", [P, TOPK * TOPK])
        cand_top = sb("cand_top", [P, TOPK])
        cand_idx = sb("cand_idx", [P, TOPK], U32)
        place = sb("place", [P, 2, TOPK], U32)
        place_f = sb("place_f", [P, 2, TOPK])
        onehot = sb("onehot", [P, 2, TOPK, TOPK])
        picked = sb("picked", [P, 2, TOPK])
        expert = sb("expert", [P, 2, TOPK], U32)
        neg_best = sb("neg_best", [P, 1])
        gate = sb("gate", [P, TOPK])
        gate_sum = sb("gate_sum", [P, 1])
        inv_gate = sb("inv_gate", [P, 1])
        hid = sb("hid", [P, TOPK])
        g1 = sb("g1", [P, TOPK])
        g2 = sb("g2", [P, TOPK])
        g3 = sb("g3", [P, TOPK])
        gelu_exp = sb("gelu_exp", [P, TOPK])
        coef = sb("coef", [P, TOPK])
        diag = sb("diag", [P, TOPK, P])

        bank = [ctx.enter_context(nc.psum_tensor(f"bank{b}", [P, BANK], F32)) for b in range(6)]
        x_cur = ctx.enter_context(nc.psum_tensor("x_cur", [P, D], F32))
        q_bank, k_bank = bank[0], bank[1]
        v_bank, o_bank = x_cur[:, 0:BANK], x_cur[:, BANK:D]
        z_bank, t_bank = [bank[2], bank[3]], [bank[4], bank[5]]
        acc = [bank[0], bank[1]]
        pq_bank, s_bank = [bank[2], bank[3]], [bank[4], bank[5]]

        x_landed = sem("x_landed")
        gain_landed = [sem("gain_landed0"), sem("gain_landed1")]
        small_landed = sem("small_landed")
        const_ready = sem("const_ready")
        pool_step = sem("pool_step")
        sumsq_ready = sem("sumsq_ready")
        root_ready = sem("root_ready")
        xn_ready = sem("xn_ready")
        xT_done = sem("xT_done")
        xnT_ready = sem("xnT_ready")
        wqkv_landed = sem("wqkv_landed")
        wkv_landed = sem("wkv_landed")
        wq_landed = sem("wq_landed")
        wo_landed = sem("wo_landed")
        proj_done = sem("proj_done")
        proj_copied = sem("proj_copied")
        z_done = sem("z_done")
        gates_ready = sem("gates_ready")
        left_ready = sem("left_ready")
        attn_ready = sem("attn_ready")
        attnT_done = sem("attnT_done")
        attnT_ready = sem("attnT_ready")
        o_done = sem("o_done")
        oT_ready = sem("oT_ready")
        wo_done = sem("wo_done")
        h_added = sem("h_added")
        ones_ready = sem("ones_ready")
        bias_ready = sem("bias_ready")
        kv_done = sem("kv_done")
        k_copied = sem("k_copied")
        kss_ready = sem("kss_ready")
        kroot_ready = sem("kroot_ready")
        kn_ready = sem("kn_ready")
        kT_done = sem("kT_done")
        kT_ready = sem("kT_ready")
        q_done = sem("q_done")
        q_copied = sem("q_copied")
        qss_ready = sem("qss_ready")
        qroot_ready = sem("qroot_ready")
        qn_ready = sem("qn_ready")
        qT_done = sem("qT_done")
        qT_ready = sem("qT_ready")
        swz_done = sem("swz_done")
        swz_read = sem("swz_read")
        negtop_ready = sem("negtop_ready")
        prob_ready = sem("prob_ready")
        probn_ready = sem("probn_ready")
        probT_done = sem("probT_done")
        probT_ready = sem("probT_ready")
        swo_done = sem("swo_done")
        swoT_ready = sem("swoT_ready")
        wpq_landed = sem("wpq_landed")
        keysT_done = sem("keysT_done")
        keysT_ready = sem("keysT_ready")
        pq_done = sem("pq_done")
        pqT_ready = sem("pqT_ready")
        score_done = sem("score_done")
        scores_ready = sem("scores_ready")
        best_ready = sem("best_ready")
        gate_ready = sem("gate_ready")
        expert_ready = sem("expert_ready")
        units_begun = sem("units_begun")
        gathers_issued = sem("gathers_issued")
        u_landed = [sem(f"u_landed{s}") for s in range(SLOTS)]
        v_landed = [sem(f"v_landed{s}") for s in range(SLOTS)]
        u_slots_free = sem("u_slots_free")
        v_slots_free = sem("v_slots_free")
        gelu_arg_ready = sem("gelu_arg_ready")
        gelu_exp_ready = sem("gelu_exp_ready")
        coef_ready = sem("coef_ready")
        diag_ready = sem("diag_ready")
        acc_stored = sem("acc_stored")
        dve_step = sem("dve_step")
        out_stored = sem("out_stored")

        block = ctx.enter_context(nc.Block())
        FIRST_PAIR_UNITS = 2 * TT

        @block.sync
        def _(sp):
            for t in range(TT):
                sp.dma_start(h[:, t, :], x_tiles[t]).then_inc(x_landed, 16)

            def load_gain(m):
                if m >= 2:
                    sp.wait_ge(xn_ready, TT * (m - 1))
                sp.dma_start(gain_b[:, m % 2, :], gains[m].broadcast_to([P, D])).then_inc(gain_landed[m % 2], 16)

            load_gain(0)
            load_gain(1)
            w3 = sb_w_qkv[0].rearrange("(k p) n -> p k n", p=P)
            with sp.Fori(0, PAIRS) as i:
                sp.wait_ge(proj_done, i * 3 + CREDIT)
                for sec, w in enumerate((w_q, w_k, w_v)):
                    sp.dma_start(w[:], w3[:, :, bass.ds(i * P + sec * D, P)]).then_inc(wqkv_landed, 16)
            sp.dma_start(wo, sb_w_o[0].rearrange("(k p) n -> p k n", p=P)).then_inc(wo_landed, 16)
            sp.dma_start(qk_gain[:, 0, :], sw_q_gain[0:1, :].broadcast_to([P, DH])).then_inc(small_landed, 16)
            sp.dma_start(qk_gain[:, 1, :], sw_k_gain[0:1, :].broadcast_to([P, DH])).then_inc(small_landed, 16)
            sp.dma_start(sink_b[:], sw_sinks[0:1, :].broadcast_to([P, SW_HEADS])).then_inc(small_landed, 16)

            def load_peer(layer):
                wq3 = peer_w_query[layer].rearrange("(k p) n -> p k n", p=P)
                sk = peer_sub_keys[layer].rearrange("h s n c -> n h s c")
                with sp.Fori(0, PEER_HEADS) as hd:
                    sp.wait_ge(pq_done, hd * 2 + (layer * 2 * PEER_HEADS + CREDIT))
                    sp.dma_start(w_pq[:], wq3[:, :, bass.ds(hd * 2 * P, 2 * P)]).then_inc(wpq_landed, 16)
                    sp.dma_start(keys[:], sk[:, bass.ds(hd, 1), :, :].squeeze(1)).then_inc(wpq_landed, 16)

            load_peer(0)
            load_gain(2)
            load_gain(3)
            w2 = sw_w_qkv[0].rearrange("(k p) n -> p k n", p=P)
            for j in range(KV_PAIRS):
                if j:
                    sp.wait_ge(kv_done, 2 * j)
                sp.dma_start(w_k[:], w2[:, :, D + j * P:D + (j + 1) * P]).then_inc(wkv_landed, 16)
                sp.dma_start(w_v[:], w2[:, :, D + (KV_PAIRS + j) * P:D + (KV_PAIRS + j + 1) * P]).then_inc(wkv_landed, 16)
                with sp.Fori(0, GROUP) as g:
                    sp.wait_ge(q_done, g + (GROUP * j + CREDIT))
                    for a in range(2):
                        col = j * 2 * GROUP * DH + a * GROUP * DH
                        sp.dma_start(w_q[:, :, a * DH:(a + 1) * DH],
                                     w2[:, :, bass.ds(g * DH + col, DH)]).then_inc(wq_landed, 16)
                if j == 0:
                    sp.wait_ge(acc_stored, UNITS + CREDIT)
                    woh = sw_w_o[0].rearrange("(j a g p) n -> a p j g n", j=KV_PAIRS, a=2, g=GROUP)
                    for a in range(2):
                        for jj in range(KV_PAIRS):
                            sp.dma_start(wo[a * DH:(a + 1) * DH, jj * GROUP:(jj + 1) * GROUP, :],
                                         woh[a][:, jj]).then_inc(wo_landed, 16)
            load_peer(1)
            sp.wait_ge(acc_stored, 2 * UNITS + CREDIT)
            for t in range(TT):
                sp.dma_start(out_tiles[t], h[:, t, :]).then_inc(out_stored, 16)
            sp.wait_ge(out_stored, 16 * TT)

        @block.gpsimd
        def _(pool):
            pool.memset(eps[:], RMS_EPS).then_inc(const_ready, 1)
            pool.memset(ident[:], 0.0).then_inc(pool_step, 1)
            pool.memset(ident_bf[:], 0.0).then_inc(pool_step, 1)
            pool.memset(later_bf[:], MASKED).then_inc(pool_step, 1)
            pool.wait_ge(pool_step, 3)
            for m in (ident, ident_bf):
                pool.affine_select(out=m[:], in_=m[:], compare_op=ALU.not_equal, fill=1.0, base=0,
                                   pattern=[[-1, P]], channel_multiplier=1).then_inc(const_ready, 1)
            pool.affine_select(out=later_bf[:], in_=later_bf[:], compare_op=ALU.is_ge, fill=0.0, base=0,
                               pattern=[[1, P]], channel_multiplier=-1).then_inc(const_ready, 1)
            pool.iota(slot_no[:], pattern=[[1, TOPK]], base=0, channel_multiplier=0,
                      allow_small_or_imprecise_dtypes=True).then_inc(const_ready, 1)
            pool.iota(dist[:], pattern=[[-1, WIN]], base=P, channel_multiplier=1,
                      allow_small_or_imprecise_dtypes=True).then_inc(const_ready, 1)
            steps = [3]

            def gathers(layer):
                with pool.Fori(0, PEER_HEADS) as hd:
                    for t in range(TT):
                        first = UNITS * layer + t
                        pool.wait_ge(expert_ready, hd * TT + (first + 1))
                        pool.sem_inc(gathers_issued, 1)
                        for table, ring, landed, free in ((peer_u, u_ring, u_landed, u_slots_free),
                                                          (peer_v, v_ring, v_landed, v_slots_free)):
                            for k in range(TOPK):
                                pool.wait_ge(free, hd * (TT * TOPK) + (first * TOPK + k + 1))
                                pool.sem_inc(gathers_issued, 1)
                                pool.indirect_dma_start(
                                    ring[:, k % SLOTS, :], None, table.rearrange("l e d -> (l e) d"),
                                    bass.IndirectOffsetOnAxis(ap=expert[:, t % 2, k:k + 1], axis=0),
                                    element_offset=layer * KEYS * KEYS * D).then_inc(landed[k % SLOTS], 16)

            with pool.Fori(0, PAIRS) as i:
                for u in range(FIRST_PAIR_UNITS):
                    w = (u % TT + 1) * P
                    r = u % RING3
                    pool.wait_ge(left_ready, i * FIRST_PAIR_UNITS + (u + 1))
                    if u >= RING3:
                        pool.wait_ge(attnT_done, i * FIRST_PAIR_UNITS + (u - RING3 + 1))
                    pool.tensor_tensor(attn[:, r, 0:w], take[:, r, 0:w], left[:, r, BANK + 1 - w:BANK + 1],
                                       ALU.mult).then_inc(attn_ready, 1)
            gathers(0)
            pool.wait_ge(acc_stored, UNITS + CREDIT)
            pool.tensor_scalar(bias[:, 0, :], dist[:], -1.0, None, ALU.mult).then_inc(pool_step, 1)
            steps[0] += 1
            pool.wait_ge(pool_step, steps[0])
            for hd in range(SW_HEADS - 1, -1, -1):
                slope = 2.0 ** (-8.0 * (hd + 1) / SW_HEADS)
                pool.tensor_scalar(bias[:, hd, :], bias[:, 0, :], slope, None, ALU.mult).then_inc(pool_step, 1)
                steps[0] += 1
                pool.wait_ge(pool_step, steps[0])
                pool.affine_select(out=bias[:, hd, :], in_=bias[:, hd, :], compare_op=ALU.is_ge, fill=MASKED,
                                   base=P, pattern=[[-1, WIN]], channel_multiplier=1).then_inc(pool_step, 1)
                steps[0] += 1
                pool.wait_ge(pool_step, steps[0])
                pool.affine_select(out=bias[:, hd, :], in_=bias[:, hd, :], compare_op=ALU.is_gt, fill=MASKED,
                                   base=0, pattern=[[1, WIN]], channel_multiplier=-1).then_inc(bias_ready, 1)
            gathers(1)

        @block.scalar
        def _(act):
            def norm(m, source, n):
                act.wait_ge(source, n)
                for t in range(TT):
                    act.activation(xn[:, t, :], h[:, t, :], ACT.Square,
                                   accum_out=sumsq[:, t:t + 1]).then_inc(sumsq_ready, 1)
                act.wait_ge(sumsq_ready, TT * (m + 1))
                act.activation(root[:], sumsq[:], ACT.Sqrt, bias=eps[:], scale=1.0 / D).then_inc(root_ready, 1)
                for t in range(TT):
                    for b in range(2):
                        act.wait_ge(xT_done, 2 * TT * m + 2 * t + b + 1)
                        act.activation(xnT[:, 4 * b:4 * b + 4, t * P:(t + 1) * P],
                                       t_bank[b][:].rearrange("p (k s) -> p k s", k=4),
                                       ACT.Copy).then_inc(xnT_ready, 1)

            def stick_breaking():
                with act.Fori(0, PAIRS) as i:
                    for n, (dst, src) in enumerate(((qT[:], q_bank[:]), (kT[:], k_bank[:]),
                                                    (v_tok[:].rearrange("p t c -> p (t c)"), v_bank))):
                        act.wait_ge(proj_done, i * 3 + (n + 1 + CREDIT))
                        act.activation(dst, src, ACT.Copy).then_inc(proj_copied, 1)
                    for u in range(FIRST_PAIR_UNITS):
                        w = (u % TT + 1) * P
                        r = u % RING3
                        act.wait_ge(z_done, i * FIRST_PAIR_UNITS + (u + 1))
                        if u >= RING3:
                            act.wait_ge(attn_ready, i * FIRST_PAIR_UNITS + (u - RING3 + 1))
                        act.activation(fail[:, r, 0:w], z_bank[u % 2][:, 0:w], ACT.Sigmoid, scale=-SCALE)
                        act.activation(take[:, r, 0:w], z_bank[u % 2][:, 0:w], ACT.Sigmoid,
                                       scale=SCALE).then_inc(gates_ready, 1)

            def window():
                for j in range(KV_PAIRS):
                    act.wait_ge(kv_done, 2 * j + 2)
                    act.activation(head_tok, k_bank[:], ACT.Copy).then_inc(k_copied, 1)
                    act.activation(head_sq, k_bank[:], ACT.Square).then_inc(k_copied, 1)
                    act.activation(v_tok[:].rearrange("p t c -> p (t c)"), v_bank, ACT.Copy).then_inc(k_copied, 1)
                    act.wait_ge(kss_ready, j + 1)
                    act.activation(head_root[:], head_ss[:], ACT.Sqrt, bias=eps[:], scale=1.0 / DH).then_inc(kroot_ready, 1)
                    act.wait_ge(kT_done, j + 1)
                    act.activation(kT[:], t_bank[0][:], ACT.Copy).then_inc(kT_ready, 1)
                    with act.Fori(0, GROUP) as g:
                        act.wait_ge(q_done, g + (GROUP * j + 1 + CREDIT))
                        act.activation(head_tok, q_bank[:], ACT.Copy).then_inc(q_copied, 1)
                        act.activation(head_sq, q_bank[:], ACT.Square).then_inc(q_copied, 1)
                        act.wait_ge(qss_ready, g + (GROUP * j + 1))
                        act.activation(head_root[:], head_ss[:], ACT.Sqrt, bias=eps[:],
                                       scale=1.0 / DH).then_inc(qroot_ready, 1)
                        act.wait_ge(qT_done, g + (GROUP * j + 1))
                        act.activation(qT[:], t_bank[1][:], ACT.Copy).then_inc(qT_ready, 1)
                        for a in range(2):
                            act.wait_ge(negtop_ready, g * 2 + (2 * GROUP * j + a + 1))
                            for n in range(TT):
                                lo = P if n == 0 else 0
                                act.activation(prob[:, a, n, lo:WIN], sc_sb[:, a, n, lo:WIN], ACT.Exp,
                                               bias=neg_top[:, a, n:n + 1], accum_out=row_sum[:, a, n:n + 1])
                            act.activation(sink_exp[:, a, :], sink_arg[:, a, :], ACT.Exp).then_inc(prob_ready, 1)

            def copy_scores(layer, hd):
                act.wait_ge(keysT_done, hd + (layer * PEER_HEADS + 1))
                act.activation(keysT[:].rearrange("p a b -> p (a b)"), s_bank[0][:, 0:2 * P],
                               ACT.Copy).then_inc(keysT_ready, 1)
                for half in range(2):
                    act.wait_ge(pq_done, hd * 2 + (layer * 2 * PEER_HEADS + half + 1 + CREDIT))
                    act.activation(pqT[:, half, :], pq_bank[half][:], ACT.Copy).then_inc(pqT_ready, 1)
                for half in range(2):
                    act.wait_ge(score_done, hd * 2 + (layer * 2 * PEER_HEADS + half + 1))
                    act.activation(scores[:, :, half, :], s_bank[half][:].rearrange("p (t n) -> p t n", t=TT),
                                   ACT.Copy).then_inc(scores_ready, 1)

            def peer_head(layer, hd, more):
                for t in range(TT):
                    unit = UNITS * layer + t
                    act.wait_ge(best_ready, hd * TT + (unit + 1))
                    act.activation(gate[:], cand_top[:], ACT.Exp, bias=neg_best[:],
                                   accum_out=gate_sum[:]).then_inc(gate_ready, 1)
                    if t == TT - 1 and more:
                        copy_scores(layer, hd + 1)
                    act.wait_ge(gelu_arg_ready, hd * TT + (unit + 1))
                    act.activation(gelu_exp[:], g3[:], ACT.Exp).then_inc(gelu_exp_ready, 1)
                    act.wait_ge(coef_ready, hd * TT + (unit + 1))
                    for k in range(TOPK):
                        act.activation(diag[:, k, :], ident[:], ACT.Copy,
                                       scale=coef[:, k:k + 1]).then_inc(diag_ready, 1)
                    act.wait_ge(v_slots_free, hd * (TT * TOPK) + ((unit + 1) * TOPK + SLOTS))
                    for c in range(HALVES):
                        ins = act.activation(h[:, t, c * BANK:(c + 1) * BANK], acc[c][:], ACT.Copy)
                    ins.then_inc(acc_stored, 1)

            def peer(layer):
                copy_scores(layer, 0)
                with act.Fori(0, PEER_HEADS - 1) as hd:
                    peer_head(layer, hd, True)
                peer_head(layer, PEER_HEADS - 1, False)

            act.sem_inc(acc_stored, CREDIT)
            act.wait_ge(const_ready, 6)
            norm(0, x_landed, 16 * TT)
            stick_breaking()
            norm(1, h_added, 2 * TT)
            peer(0)
            norm(2, acc_stored, UNITS + CREDIT)
            window()
            norm(3, h_added, 4 * TT)
            peer(1)

        @block.tensor
        def _(pe):
            def norm(m):
                for t in range(TT):
                    pe.wait_ge(xn_ready, TT * m + t + 1)
                    for b in range(2):
                        if t >= 1:
                            pe.wait_ge(xnT_ready, 2 * TT * m + 2 * (t - 1) + b + 1)
                        for k in range(4):
                            ins = pe.transpose(t_bank[b][:, k * P:(k + 1) * P],
                                               xn[:, t, (4 * b + k) * P:(4 * b + k + 1) * P], ident[:])
                        ins.then_inc(xT_done, 1)

            def project_T(dst, w):
                for k in range(KC):
                    ins = pe.matmul(dst, w[:, k, :], xnT[:, k, :], start=(k == 0), stop=(k == KC - 1))
                return ins

            def project(dst, w):
                for t in range(TT):
                    for k in range(KC):
                        ins = pe.matmul(dst[:, t * P:(t + 1) * P], xnT[:, k, t * P:(t + 1) * P], w[:, k, :],
                                        start=(k == 0), stop=(k == KC - 1))
                return ins

            def stick_breaking():
                pe.wait_ge(xnT_ready, 2 * TT)
                with pe.Fori(0, PAIRS) as i:
                    pe.wait_ge(wqkv_landed, i * 48 + 48)
                    project_T(q_bank[:], w_q).then_inc(proj_done, 1)
                    project_T(k_bank[:], w_k).then_inc(proj_done, 1)
                    project(v_bank, w_v).then_inc(proj_done, 1)
                    pe.wait_ge(proj_copied, i * 3 + 3)
                    for step in range(FIRST_PAIR_UNITS + 3):
                        u = step
                        if u < FIRST_PAIR_UNITS:
                            a, n = u // TT, u % TT
                            rows = slice(a * DH, (a + 1) * DH)
                            if u >= 2:
                                pe.wait_ge(gates_ready, i * FIRST_PAIR_UNITS + (u - 1))
                            pe.matmul(z_bank[u % 2][:, 0:(n + 1) * P], qT[rows, n * P:(n + 1) * P],
                                      kT[rows, 0:(n + 1) * P], start=True, stop=False, skip_group_check=True)
                            pe.matmul(z_bank[u % 2][:, n * P:(n + 1) * P], ident_bf[:], later_bf[:],
                                      start=False, stop=True, skip_group_check=True).then_inc(z_done, 1)
                        u = step - 2
                        if 0 <= u < FIRST_PAIR_UNITS:
                            n = u % TT
                            pe.wait_ge(attn_ready, i * FIRST_PAIR_UNITS + (u + 1))
                            if u >= 2:
                                pe.wait_ge(attnT_ready, i * FIRST_PAIR_UNITS + (u - 1))
                            for kb in range(n + 1):
                                ins = pe.transpose(t_bank[u % 2][:, kb * P:(kb + 1) * P],
                                                   attn[:, u % RING3, kb * P:(kb + 1) * P], ident[:])
                            ins.then_inc(attnT_done, 1)
                        u = step - 3
                        if 0 <= u < FIRST_PAIR_UNITS:
                            a, n = u // TT, u % TT
                            rows = slice(a * DH, (a + 1) * DH)
                            if u == 0:
                                pe.wait_ge(oT_ready, i + CREDIT)
                            pe.wait_ge(attnT_ready, i * FIRST_PAIR_UNITS + (u + 1))
                            for kb in range(n + 1):
                                ins = pe.matmul(o_bank[rows, n * P:(n + 1) * P], v_tok[:, kb, rows],
                                                attnT[:, u % 2, kb * P:(kb + 1) * P],
                                                start=(kb == 0), stop=(kb == n))
                            ins.then_inc(o_done, 1)

            def window():
                pe.wait_ge(xnT_ready, 3 * 2 * TT)
                for j in range(KV_PAIRS):
                    pe.wait_ge(wkv_landed, 32 * (j + 1))
                    project(k_bank, w_k).then_inc(kv_done, 1)
                    project(v_bank, w_v).then_inc(kv_done, 1)
                    pe.wait_ge(kn_ready, j + 1)
                    for t in range(TT):
                        ins = pe.transpose(t_bank[0][:, t * P:(t + 1) * P], head_tok[:, t * P:(t + 1) * P], ident[:])
                    ins.then_inc(kT_done, 1)
                    pe.wait_ge(kT_ready, j + 1)
                    pe.wait_ge(k_copied, 3 * (j + 1))
                    with pe.Fori(0, GROUP) as g:
                        pe.wait_ge(wq_landed, g * 32 + 32 * (GROUP * j + 1))
                        project(q_bank, w_q).then_inc(q_done, 1)
                        pe.wait_ge(qn_ready, g + (GROUP * j + 1))
                        for t in range(TT):
                            ins = pe.transpose(t_bank[1][:, t * P:(t + 1) * P], head_tok[:, t * P:(t + 1) * P],
                                               ident[:])
                        ins.then_inc(qT_done, 1)
                        pe.wait_ge(qT_ready, g + (GROUP * j + 1))

                        def score(a):
                            rows = slice(a * DH, (a + 1) * DH)
                            if a:
                                pe.wait_ge(swz_read, g * 2 + (2 * GROUP * j + a))
                            for n in range(TT):
                                lo = P if n == 0 else 0
                                ins = pe.matmul(z_bank[n // 2][:, (n % 2) * WIN + lo:(n % 2 + 1) * WIN],
                                                qT[rows, n * P:(n + 1) * P], kT[rows, (n - 1) * P + lo:(n + 1) * P],
                                                start=True, stop=True)
                            ins.then_inc(swz_done, 1)

                        def apply(a):
                            rows = slice(a * DH, (a + 1) * DH)
                            pe.wait_ge(probn_ready, g * 2 + (2 * GROUP * j + a + 1))
                            for n in range(TT):
                                for b in range(2 if n else 1):
                                    c = (n % 2) * WIN + b * P
                                    src = b if n else 1
                                    ins = pe.transpose(t_bank[n // 2][:, c:c + P],
                                                       prob[:, a, n, src * P:(src + 1) * P], ident[:])
                            ins.then_inc(probT_done, 1)
                            pe.wait_ge(probT_ready, g * 2 + (2 * GROUP * j + a + 1))
                            for n in range(TT):
                                blocks = [n - 1, n] if n else [0]
                                for b, kb in enumerate(blocks):
                                    c = n * WIN + b * P
                                    ins = pe.matmul(o_bank[rows, n * P:(n + 1) * P], v_tok[:, kb, rows],
                                                    attnT[:, a, c:c + P], start=(b == 0),
                                                    stop=(b == len(blocks) - 1))
                            ins.then_inc(swo_done, 1)

                        score(0)
                        score(1)
                        pe.wait_ge(swoT_ready, g + (GROUP * j + CREDIT))
                        apply(0)
                        apply(1)

            def output(layer, ready):
                pe.wait_ge(wo_landed, 16 + 64 * layer)
                pe.wait_ge(ready, PAIRS + CREDIT)
                for n in range(TT * HALVES):
                    t, c = n // HALVES, n % HALVES
                    if n >= 2:
                        pe.wait_ge(h_added, 2 * TT * layer + n - 1)
                    for k in range(KC):
                        ins = pe.matmul(z_bank[n % 2][:], oT_all[:, k, t * P:(t + 1) * P],
                                        wo[:, k, c * BANK:(c + 1) * BANK], start=(k == 0), stop=(k == KC - 1))
                    ins.then_inc(wo_done, 1)

            def score_head(layer, hd):
                pe.wait_ge(wpq_landed, hd * 32 + 32 * (layer * PEER_HEADS + 1))
                for half in range(2):
                    ins = pe.transpose(s_bank[0][:, half * P:(half + 1) * P], keys[:, half, :], ident[:])
                ins.then_inc(keysT_done, 1)
                for half in range(2):
                    for k in range(KC):
                        ins = pe.matmul(pq_bank[half][:], w_pq[:, k, half * P:(half + 1) * P], xnT[:, k, :],
                                        start=(k == 0), stop=(k == KC - 1))
                    ins.then_inc(pq_done, 1)
                pe.wait_ge(keysT_ready, hd + (layer * PEER_HEADS + 1))
                for half in range(2):
                    pe.wait_ge(pqT_ready, hd * 2 + (layer * 2 * PEER_HEADS + half + 1))
                    for t in range(TT):
                        ins = pe.matmul(s_bank[half][:, t * P:(t + 1) * P], pqT[:, half, t * P:(t + 1) * P],
                                        keysT[:, half, :], start=True, stop=True)
                    ins.then_inc(score_done, 1)

            def peer_head(layer, hd, more):
                for t in range(TT):
                    if t == TT - 1 and more:
                        score_head(layer, hd + 1)
                    unit = UNITS * layer + t
                    pe.wait_ge(acc_stored, hd * TT + (unit + CREDIT))
                    for c in range(HALVES):
                        ins = pe.matmul(acc[c][:], ident[:], h[:, t, c * BANK:(c + 1) * BANK],
                                        start=True, stop=False, skip_group_check=True)
                    ins.then_inc(units_begun, 1)
                    for k in range(TOPK):
                        pe.wait_ge(v_landed[k % SLOTS],
                                   hd * (TT * 32) + (unit * 32 + 16 * (k // SLOTS + 1)))
                        pe.wait_ge(diag_ready, hd * (TT * TOPK) + (unit * TOPK + k + 1))
                        for c in range(HALVES):
                            ins = pe.matmul(acc[c][:], diag[:, k, :], v_ring[:, k % SLOTS, c * BANK:(c + 1) * BANK],
                                            start=False, stop=(k == TOPK - 1), skip_group_check=True)
                        ins.then_inc(v_slots_free, 1)

            def peer(layer):
                pe.wait_ge(xnT_ready, (2 * layer + 2) * 2 * TT)
                score_head(layer, 0)
                with pe.Fori(0, PEER_HEADS - 1) as hd:
                    peer_head(layer, hd, True)
                peer_head(layer, PEER_HEADS - 1, False)

            pe.sem_inc(v_slots_free, SLOTS)
            for s in (proj_done, q_done, pq_done, units_begun):
                pe.sem_inc(s, CREDIT)
            pe.wait_ge(const_ready, 6)
            norm(0)
            stick_breaking()
            output(0, oT_ready)
            norm(1)
            peer(0)
            norm(2)
            window()
            output(1, swoT_ready)
            norm(3)
            peer(1)

        @block.vector
        def _(dve):
            def norm(m):
                dve.wait_ge(root_ready, m + 1)
                dve.sem_clear(dve_step)
                dve.reciprocal(rstd[:], root[:]).then_inc(dve_step, 1)
                dve.wait_ge(dve_step, 1)
                dve.wait_ge(gain_landed[m % 2], 16 * (m // 2 + 1))
                for t in range(TT):
                    dve.scalar_tensor_tensor(out=xn[:, t, :], in0=h[:, t, :], scalar=rstd[:, t:t + 1],
                                             in1=gain_b[:, m % 2, :], op0=ALU.mult,
                                             op1=ALU.mult).then_inc(xn_ready, 1)

            def stick_breaking():
                dve.memset(left[:, :, BANK:BANK + 1], 1.0).then_inc(ones_ready, 1)
                dve.wait_ge(ones_ready, 1)
                with dve.Fori(0, PAIRS) as i:
                    for step in range(FIRST_PAIR_UNITS + 2):
                        u = step
                        if u < FIRST_PAIR_UNITS:
                            w = (u % TT + 1) * P
                            r = u % RING3
                            dve.wait_ge(gates_ready, i * FIRST_PAIR_UNITS + (u + 1))
                            if u >= RING3:
                                dve.wait_ge(attn_ready, i * FIRST_PAIR_UNITS + (u - RING3 + 1))
                            dve.tensor_tensor_scan(left[:, r, BANK - w:BANK][:, ::-1], fail[:, r, 0:w][:, ::-1],
                                                   fail[:, r, 0:w][:, ::-1], 1.0, ALU.mult,
                                                   ALU.bypass).then_inc(left_ready, 1)
                        u = step - 2
                        if 0 <= u < FIRST_PAIR_UNITS:
                            w = (u % TT + 1) * P
                            dve.wait_ge(attnT_done, i * FIRST_PAIR_UNITS + (u + 1))
                            if u >= 2:
                                dve.wait_ge(o_done, i * FIRST_PAIR_UNITS + (u - 1))
                            dve.tensor_copy(attnT[:, u % 2, 0:w], t_bank[u % 2][:, 0:w]).then_inc(attnT_ready, 1)
                    dve.wait_ge(o_done, i * FIRST_PAIR_UNITS + FIRST_PAIR_UNITS)
                    dve.tensor_copy(oT_all[:, bass.ds(i, 1), :].squeeze(1), o_bank).then_inc(oT_ready, 1)

            def window():
                dve.wait_ge(small_landed, 48)
                dve.wait_ge(bias_ready, SW_HEADS)
                dve.memset(sc_sb[:, :, 0, 0:P], MASKED).then_inc(ones_ready, 1)
                dve.memset(prob[:, :, 0, 0:P], 0.0).then_inc(ones_ready, 1)
                dve.wait_ge(ones_ready, 3)
                tok = head_tok.rearrange("p (n c) -> p n c", c=DH)

                def head_norm(which, copied, n_copied, ss_ready, rs_ready, n, done):
                    dve.wait_ge(copied, n_copied)
                    dve.tensor_reduce(head_ss[:], head_sq.rearrange("p (n c) -> p n c", c=DH), AX_X,
                                      ALU.add).then_inc(ss_ready, 1)
                    dve.sem_clear(dve_step)
                    dve.wait_ge(rs_ready, n)
                    dve.reciprocal(head_rstd[:], head_root[:]).then_inc(dve_step, 1)
                    dve.wait_ge(dve_step, 1)
                    dve.tensor_tensor(tok, tok, spread(head_rstd[:], 2, [P, 2 * TT, DH]), ALU.mult).then_inc(dve_step, 1)
                    dve.wait_ge(dve_step, 2)
                    dve.tensor_tensor(tok, tok, spread(qk_gain[:, which, :], 1, [P, 2 * TT, DH]),
                                      ALU.mult).then_inc(done, 1)

                for j in range(KV_PAIRS):
                    head_norm(1, k_copied, 3 * j + 2, kss_ready, kroot_ready, j + 1, kn_ready)
                    with dve.Fori(0, GROUP) as g:
                        head_norm(0, q_copied, g * 2 + 2 * (GROUP * j + 1), qss_ready, qroot_ready,
                                  g + (GROUP * j + 1), qn_ready)
                        for a in range(2):
                            hd = g + (2 * GROUP * j + GROUP * a)
                            head_bias = bias[:, bass.ds(hd, 1), :]
                            dve.wait_ge(swz_done, g * 2 + (2 * GROUP * j + a + 1))
                            dve.scalar_tensor_tensor(out=sc_sb[:, a, 0, P:WIN], in0=z_bank[0][:, P:WIN], scalar=SCALE,
                                                     in1=head_bias[:, 0, P:WIN], op0=ALU.mult, op1=ALU.add)
                            dve.scalar_tensor_tensor(out=sc_sb[:, a, 1, :], in0=z_bank[0][:, WIN:2 * WIN], scalar=SCALE,
                                                     in1=head_bias[:, 0, :], op0=ALU.mult, op1=ALU.add)
                            dve.sem_clear(dve_step)
                            dve.scalar_tensor_tensor(out=sc_sb[:, a, 2:4, :],
                                                     in0=z_bank[1][:].rearrange("p (n w) -> p n w", n=2),
                                                     scalar=SCALE, in1=head_bias.broadcast_to([P, 2, WIN]),
                                                     op0=ALU.mult, op1=ALU.add).then_inc(swz_read, 1)
                            dve.wait_ge(swz_read, g * 2 + (2 * GROUP * j + a + 1))
                            dve.tensor_reduce(top[:, a, :], sc_sb[:, a, :, :], AX_X, ALU.max).then_inc(dve_step, 1)
                            dve.wait_ge(dve_step, 1)
                            sink = sink_b[:, bass.ds(hd, 1)]
                            dve.tensor_scalar(neg_top[:, a, :], top[:, a, :], sink, -1.0, ALU.max,
                                              ALU.mult).then_inc(dve_step, 1)
                            dve.wait_ge(dve_step, 2)
                            dve.tensor_scalar(sink_arg[:, a, :], neg_top[:, a, :], sink, None,
                                              ALU.add).then_inc(negtop_ready, 1)
                        for a in range(2):
                            dve.sem_clear(dve_step)
                            dve.wait_ge(prob_ready, g * 2 + (2 * GROUP * j + a + 1))
                            dve.tensor_tensor(denom[:, a, :], row_sum[:, a, :], sink_exp[:, a, :],
                                              ALU.add).then_inc(dve_step, 1)
                            dve.wait_ge(dve_step, 1)
                            dve.reciprocal(inv_denom[:, a, :], denom[:, a, :]).then_inc(dve_step, 1)
                            dve.wait_ge(dve_step, 2)
                            dve.tensor_tensor(prob[:, a, :, :], prob[:, a, :, :],
                                              spread(inv_denom[:, a, :], 2, [P, TT, WIN]),
                                              ALU.mult).then_inc(probn_ready, 1)
                        for a in range(2):
                            dve.wait_ge(probT_done, g * 2 + (2 * GROUP * j + a + 1))
                            dve.tensor_copy(attnT[:, a, 0:P], t_bank[0][:, 0:P])
                            dve.tensor_copy(attnT[:, a, WIN:2 * WIN], t_bank[0][:, WIN:2 * WIN])
                            dve.tensor_copy(attnT[:, a, 2 * WIN:4 * WIN], t_bank[1][:]).then_inc(probT_ready, 1)
                        dve.wait_ge(swo_done, g * 2 + (2 * GROUP * j + 2))
                        dve.tensor_copy(oT_all[:, bass.ds(g + GROUP * j, 1), :].squeeze(1),
                                        o_bank).then_inc(swoT_ready, 1)

            def output(layer):
                for n in range(TT * HALVES):
                    t, c = n // HALVES, n % HALVES
                    dve.wait_ge(wo_done, 2 * TT * layer + n + 1)
                    part = h[:, t, c * BANK:(c + 1) * BANK]
                    dve.tensor_tensor(part, z_bank[n % 2][:], part, ALU.add).then_inc(h_added, 1)

            def top16(values, others, top_out, idx_out, step):
                step(dve.max(top_out[:, 0:TOP8], values))
                step(dve.match_replace(others, top_out[:, 0:TOP8], values, LOWEST))
                step(dve.max(top_out[:, TOP8:TOPK], others))
                dve.max_index(idx_out[:, 0:TOP8], top_out[:, 0:TOP8], values)
                step(dve.max_index(idx_out[:, TOP8:TOPK], top_out[:, TOP8:TOPK], others))

            def peer(layer):
                with dve.Fori(0, PEER_HEADS) as hd:
                    for t in range(TT):
                        unit = UNITS * layer + t
                        dve.sem_clear(dve_step)
                        count = [0]
                        if t == 0:
                            dve.wait_ge(scores_ready, hd * 2 + 2 * (layer * PEER_HEADS + 1))
                            dve.sem_inc(dve_step, 1)
                            count[0] = 1

                        def step(ins):
                            count[0] += 1
                            ins.then_inc(dve_step, 1)
                            dve.wait_ge(dve_step, count[0])

                        for half in range(2):
                            top16(scores[:, t, half, :], rest[:, half, :], half_top[:, half, :],
                                  half_idx[:, half, :], step)
                        step(dve.tensor_tensor(cand[:], spread(half_top[:, 0, :], 2, [P, TOPK, TOPK]),
                                               spread(half_top[:, 1, :], 1, [P, TOPK, TOPK]), ALU.add))
                        cand_flat = cand[:].rearrange("p a b -> p (a b)")
                        top16(cand_flat, cand_rest[:], cand_top[:], cand_idx[:], step)
                        dve.tensor_scalar(neg_best[:], cand_top[:, 0:1], -1.0, None, ALU.mult).then_inc(best_ready, 1)
                        dve.tensor_copy(half_idx_f[:], half_idx[:])
                        dve.tensor_single_scalar(place[:, 0, :], cand_idx[:], 4, ALU.logical_shift_right)
                        step(dve.tensor_single_scalar(place[:, 1, :], cand_idx[:], TOPK - 1, ALU.bitwise_and))
                        step(dve.tensor_copy(place_f[:], place[:]))
                        shape = [P, 2, TOPK, TOPK]
                        step(dve.tensor_tensor(onehot[:], spread(place_f[:], 3, shape),
                                               slot_no[:].unsqueeze(1).unsqueeze(1).broadcast_to(shape), ALU.is_equal))
                        step(dve.tensor_tensor(onehot[:], onehot[:], spread(half_idx_f[:], 2, shape), ALU.mult))
                        step(dve.tensor_reduce(picked[:], onehot[:], AX_X, ALU.add))
                        dve.wait_ge(units_begun, hd * TT + (unit + CREDIT))
                        dve.scalar_tensor_tensor(out=expert[:, t % 2, :], in0=picked[:, 0, :], scalar=float(KEYS),
                                                 in1=picked[:, 1, :], op0=ALU.mult,
                                                 op1=ALU.add).then_inc(expert_ready, 1)
                        step(dve.tensor_copy(x_cur[:], xn[:, t, :]))
                        for k in range(TOPK):
                            dve.wait_ge(u_landed[k % SLOTS], hd * (TT * 32) + (unit * 32 + 16 * (k // SLOTS + 1)))
                            row = u_ring[:, k % SLOTS, :]
                            dve.tensor_tensor_reduce(row, row, x_cur[:], 1.0, 0.0, ALU.mult, ALU.add,
                                                     hid[:, k:k + 1]).then_inc(u_slots_free, 1)
                        dve.wait_ge(u_slots_free, hd * (TT * TOPK) + ((unit + 1) * TOPK + SLOTS))
                        step(dve.tensor_tensor(g1[:], hid[:], hid[:], ALU.mult))
                        step(dve.tensor_scalar(g2[:], g1[:], -GELU_C * GELU_A, -GELU_C, ALU.mult, ALU.add))
                        dve.tensor_tensor(g3[:], g2[:], hid[:], ALU.mult).then_inc(gelu_arg_ready, 1)
                        dve.wait_ge(gate_ready, hd * TT + (unit + 1))
                        dve.reciprocal(inv_gate[:], gate_sum[:])
                        dve.wait_ge(gelu_exp_ready, hd * TT + (unit + 1))
                        step(dve.tensor_scalar(g1[:], gelu_exp[:], HUGE, 1.0, ALU.min, ALU.add))
                        step(dve.reciprocal(g2[:], g1[:]))
                        step(dve.tensor_tensor(g1[:], hid[:], g2[:], ALU.mult))
                        dve.scalar_tensor_tensor(out=coef[:], in0=g1[:], scalar=inv_gate[:], in1=gate[:],
                                                 op0=ALU.mult, op1=ALU.mult).then_inc(coef_ready, 1)

            dve.sem_inc(u_slots_free, SLOTS)
            for s in (oT_ready, swoT_ready):
                dve.sem_inc(s, CREDIT)
            norm(0)
            stick_breaking()
            output(0)
            norm(1)
            peer(0)
            norm(2)
            window()
            output(1)
            norm(3)
            peer(1)


_INS = ['x', 'sb_norm', 'sb_w_qkv', 'sb_w_o', 'sw_norm', 'sw_w_qkv', 'sw_q_gain', 'sw_k_gain', 'sw_sinks', 'sw_w_o',
        'ffn_norm', 'peer_w_query', 'peer_sub_keys', 'peer_u', 'peer_v']
_OUT = ((1, S, D), 'float32')


def kernel(**inputs):
    import concourse.bacc as bacc
    from concourse.bass_utils import run_bass_kernel_spmd

    nc = bacc.Bacc("TRN2", target_bir_lowering=False, num_devices=1)
    arrays, args = {}, []
    for name in _INS:
        a = np.ascontiguousarray(inputs[name])
        arrays[f"in_{name}"] = a
        args.append(nc.dram_tensor(f"in_{name}", a.shape, mybir.dt.from_np(a.dtype), kind="ExternalInput").ap())
    shape, dtype = _OUT
    args.append(nc.dram_tensor("out_h", shape, mybir.dt.from_np(np.dtype(dtype)), kind="ExternalOutput").ap())
    build(nc, *args)
    r = run_bass_kernel_spmd(nc, [arrays], core_ids=[0])
    return r.results[0]["out_h"]
```

```python
from contextlib import ExitStack

import concourse.bass as bass
import numpy as np
from concourse import mybir

F32 = mybir.dt.float32
BF16 = mybir.dt.bfloat16
U32 = mybir.dt.uint32
ALU = mybir.AluOpType
ACT = mybir.ActivationFunctionType
AX_X = mybir.AxisListType.X

P = 128
D = 1024
S = 512
TT = S // P
NT = 2
NS = NT * P
KC = D // P
BANK = 512
HALVES = D // BANK
DH = 64
SCALE = DH ** -0.5
PAIRS = D // P
STEPS = 2 * NT
KV_PAIRS = 2
GROUP = 4
SW_HEADS = 16
WIN = 2 * P
PEER_HEADS = 8
KEYS = 128
TOPK = 16
TOP8 = 8
STAGES = 4
UNITS = PEER_HEADS * NT
SLOTS = 8
CREDIT = 1
RMS_EPS = 1e-6
MASKED = -1.0e30
LOWEST = -3.0e38
HUGE = 3.0e37
GELU_C = 2.0 * (2.0 / np.pi) ** 0.5
GELU_A = 0.044715


def spread(ap, axis, shape):
    return ap.unsqueeze(axis).broadcast_to(shape)


def first_tile(s):
    return NT * (s % 2)


def segments(s):
    return [(0, 1), (1, 4), (4, 5), (5, 7), (7, 8)] if s in (1, 2) else [(0, 1), (1, 7), (7, 8)]


def build(nc, x, sb_norm, sb_w_qkv, sb_w_o, sw_norm, sw_w_qkv, sw_q_gain, sw_k_gain, sw_sinks, sw_w_o,
          ffn_norm, peer_w_query, peer_sub_keys, peer_u, peer_v, out):
    x_tiles = x[0].rearrange("(t p) d -> t p d", p=P)
    out_tiles = out[0].rearrange("(t p) d -> t p d", p=P)
    kv_kept = nc.dram_tensor("kv_kept", (PAIRS, P, 2, NS), F32, kind="Internal").ap()

    with ExitStack() as ctx:
        def sb(name, shape, dt=F32):
            return ctx.enter_context(nc.sbuf_tensor(name, shape, dt))

        def sem(name):
            return ctx.enter_context(nc.semaphore(name))

        h = sb("h", [P, TT, D])
        xn = sb("xn", [P, TT, D])
        attn_xT = sb("attn_xT", [P, KC, NS])
        peer_xT = sb("peer_xT", [P, KC, NS])
        gain_b = sb("gain_b", [P, 2, D])
        sumsq = sb("sumsq", [P, NT])
        root = sb("root", [P, NT])
        rstd = sb("rstd", [P, NT])
        eps = sb("eps", [P, 1])
        ident = sb("ident", [P, P])
        ident_bf = sb("ident_bf", [P, P], BF16)
        later_bf = sb("later_bf", [P, P], BF16)
        slot_no = sb("slot_no", [P, TOPK])
        dist = sb("dist", [P, WIN])
        neg_slope = sb("neg_slope", [P, SW_HEADS])
        w_q = sb("w_q", [P, KC, P])
        w_k = sb("w_k", [P, KC, P])
        w_v = sb("w_v", [P, KC, P])
        wo = sb("wo", [P, D])
        qT = sb("qT", [P, NS])
        kT = sb("kT", [P, S])
        v_tok = sb("v_tok", [P, TT, P])
        oT = sb("oT", [P, NS])
        work = sb("work", [P, 8 * BANK + 2])
        fail = work[:, 0:2 * BANK].rearrange("p (r s) -> p r s", r=2)
        take = work[:, 2 * BANK:4 * BANK].rearrange("p (r s) -> p r s", r=2)
        attn = work[:, 4 * BANK:6 * BANK].rearrange("p (r s) -> p r s", r=2)
        left = work[:, 6 * BANK:8 * BANK + 2].rearrange("p (r s) -> p r s", r=2)
        sw_score = work[:, 0:2 * BANK].rearrange("p (a n w) -> p a n w", a=2, n=NT)
        prob = work[:, 2 * BANK:4 * BANK].rearrange("p (a n w) -> p a n w", a=2, n=NT)
        head_tok = work[:, 4 * BANK:5 * BANK]
        head_sq = work[:, 5 * BANK:6 * BANK]
        attnT = sb("attnT", [P, 2, BANK])
        kT_win = sb("kT_win", [P, KV_PAIRS, (NT + 1) * P])
        v_win = sb("v_win", [P, KV_PAIRS, NT + 1, P])
        qk_gain = sb("qk_gain", [P, 2, DH])
        sink_b = sb("sink_b", [P, SW_HEADS])
        head_ss = sb("head_ss", [P, 4 * NT])
        head_root = sb("head_root", [P, 4 * NT])
        head_rstd = sb("head_rstd", [P, 4 * NT])
        top = sb("top", [P, 2, NT])
        neg_top = sb("neg_top", [P, 2, NT])
        sink_arg = sb("sink_arg", [P, 2, NT])
        sink_exp = sb("sink_exp", [P, 2, NT])
        row_sum = sb("row_sum", [P, 2, NT])
        denom = sb("denom", [P, 2, NT])
        inv_denom = sb("inv_denom", [P, 2, NT])
        u_ring = sb("u_ring", [P, SLOTS, D])
        v_ring = sb("v_ring", [P, SLOTS, D])
        w_pq = sb("w_pq", [P, KC, 2 * P])
        keys = sb("keys", [P, 2, P])
        keysT = sb("keysT", [P, 2, P])
        pqT = sb("pqT", [P, 2, NS])
        scores = sb("scores", [P, NT, 2, KEYS])
        rest = sb("rest", [P, 2, KEYS])
        half_top = sb("half_top", [P, 2, TOPK])
        half_idx = sb("half_idx", [P, 2, TOPK], U32)
        half_idx_f = sb("half_idx_f", [P, 2, TOPK])
        cand = sb("cand", [P, TOPK, TOPK])
        cand_rest = sb("cand_rest", [P, TOPK * TOPK])
        cand_top = sb("cand_top", [P, TOPK])
        cand_idx = sb("cand_idx", [P, TOPK], U32)
        place = sb("place", [P, 2, TOPK], U32)
        place_f = sb("place_f", [P, 2, TOPK])
        onehot = sb("onehot", [P, 2, TOPK, TOPK])
        picked = sb("picked", [P, 2, TOPK])
        expert = sb("expert", [P, NT, TOPK], U32)
        neg_best = sb("neg_best", [P, 1])
        gate = sb("gate", [P, TOPK])
        gate_sum = sb("gate_sum", [P, 1])
        inv_gate = sb("inv_gate", [P, 1])
        hid = sb("hid", [P, TOPK])
        g1 = sb("g1", [P, TOPK])
        g2 = sb("g2", [P, TOPK])
        g3 = sb("g3", [P, TOPK])
        gelu_exp = sb("gelu_exp", [P, TOPK])
        coef = sb("coef", [P, TOPK])
        diag = sb("diag", [P, TOPK, P])

        acc = [ctx.enter_context(nc.psum_tensor(f"acc{c}", [P, BANK], F32)) for c in range(HALVES)]
        x_cur = ctx.enter_context(nc.psum_tensor("x_cur", [P, D], F32))
        qk_bank = ctx.enter_context(nc.psum_tensor("qk_bank", [P, BANK], F32))
        vo_bank = ctx.enter_context(nc.psum_tensor("vo_bank", [P, BANK], F32))
        z_own = ctx.enter_context(nc.psum_tensor("z_bank", [P, BANK], F32))
        t_own = ctx.enter_context(nc.psum_tensor("t_bank", [P, BANK], F32))
        o_part = vo_bank[:, NS:2 * NS]
        z_banks = {0: [z_own[:], acc[0][:]], 1: [z_own[:]] * 2}
        t_banks = {0: [t_own[:], acc[1][:]], 1: [t_own[:]] * 2}

        x_landed = sem("x_landed")
        attn_gain_landed = sem("attn_gain_landed")
        peer_gain_landed = sem("peer_gain_landed")
        small_landed = sem("small_landed")
        pool_step = sem("pool_step")
        const_ready = sem("const_ready")
        sumsq_ready = sem("sumsq_ready")
        root_ready = sem("root_ready")
        xn_ready = sem("xn_ready")
        xT_done = sem("xT_done")
        xT_ready = sem("xT_ready")
        wqkv_landed = sem("wqkv_landed")
        kept_landed = sem("kept_landed")
        kv_stored = sem("kv_stored")
        wo_landed = [sem("wo_landed0"), sem("wo_landed1")]
        proj_done = sem("proj_done")
        proj_copied = sem("proj_copied")
        z_done = sem("z_done")
        gates_ready = sem("gates_ready")
        left_ready = sem("left_ready")
        attn_ready = sem("attn_ready")
        attnT_done = sem("attnT_done")
        attnT_ready = sem("attnT_ready")
        o_done = sem("o_done")
        oT_ready = sem("oT_ready")
        wo_done = sem("wo_done")
        h_added = sem("h_added")
        dve_set = sem("dve_set")
        wkv_landed = sem("wkv_landed")
        wq_landed = sem("wq_landed")
        q_done = sem("q_done")
        kv_done = sem("kv_done")
        q_copied = sem("q_copied")
        v_copied = sem("v_copied")
        kept_copied = sem("kept_copied")
        headss_ready = sem("headss_ready")
        headroot_ready = sem("headroot_ready")
        headn_ready = sem("headn_ready")
        headT_done = sem("headT_done")
        headT_ready = sem("headT_ready")
        swz_done = sem("swz_done")
        swz_read = sem("swz_read")
        negtop_ready = sem("negtop_ready")
        exp_ready = sem("exp_ready")
        prob_ready = sem("prob_ready")
        probT_done = sem("probT_done")
        probT_ready = sem("probT_ready")
        swo_done = sem("swo_done")
        swoT_ready = sem("swoT_ready")
        wpq_landed = sem("wpq_landed")
        keysT_done = sem("keysT_done")
        keysT_ready = sem("keysT_ready")
        pq_done = sem("pq_done")
        pqT_ready = sem("pqT_ready")
        score_done = sem("score_done")
        scores_ready = sem("scores_ready")
        best_ready = sem("best_ready")
        gate_ready = sem("gate_ready")
        expert_ready = sem("expert_ready")
        gathers_issued = sem("gathers_issued")
        u_landed = [sem(f"u_landed{s}") for s in range(SLOTS)]
        v_landed = [sem(f"v_landed{s}") for s in range(SLOTS)]
        u_slots_free = sem("u_slots_free")
        v_slots_free = sem("v_slots_free")
        gelu_arg_ready = sem("gelu_arg_ready")
        gelu_exp_ready = sem("gelu_exp_ready")
        coef_ready = sem("coef_ready")
        diag_ready = sem("diag_ready")
        acc_added = sem("acc_added")
        dve_step = sem("dve_step")
        out_stored = sem("out_stored")

        block = ctx.enter_context(nc.Block())

        def nth(p, i):
            return i + PAIRS * (p % 2)

        def run(eng, s, iteration):
            for lo, hi in segments(s):
                if hi - lo == 1:
                    iteration(lo, lo == 0, hi == PEER_HEADS, lo)
                else:
                    with eng.Fori(lo, hi) as hd:
                        iteration(hd, False, False, lo)

        @block.sync
        def _(sp):
            w3 = sb_w_qkv[0].rearrange("(k p) n -> p k n", p=P)
            w2 = sw_w_qkv[0].rearrange("(k p) n -> p k n", p=P)
            wo0 = sb_w_o[0].rearrange("(i p) n -> p i n", p=P)
            wo1 = sw_w_o[0].rearrange("(j a g p) n -> a p j g n", j=KV_PAIRS, a=2, g=GROUP)

            def load_peer(s, hd):
                wq3 = peer_w_query[s // 2].rearrange("(k p) n -> p k n", p=P)
                sk = peer_sub_keys[s // 2].rearrange("h s n c -> n h s c")
                sp.wait_ge(pq_done, hd * 2 + (s * 2 * PEER_HEADS + CREDIT))
                sp.dma_start(w_pq[:], wq3[:, :, bass.ds(hd * 2 * P, 2 * P)]).then_inc(wpq_landed, 16)
                sp.dma_start(keys[:], sk[:, bass.ds(hd, 1), :, :].squeeze(1)).then_inc(wpq_landed, 16)

            def load_pair0(p, i):
                sp.wait_ge(proj_done, i * 3 + (24 * p + CREDIT))
                for sec, w in enumerate((w_q, w_k, w_v)):
                    sp.dma_start(w[:], w3[:, :, bass.ds(i * P + sec * D, P)]).then_inc(wqkv_landed, 16)
                if p:
                    sp.wait_ge(o_done, i * STEPS + STEPS * PAIRS)
                    kept = kv_kept[bass.ds(i, 1)].squeeze(0)
                    sp.dma_start(kT[:, 0:NS], kept[:, 0, :]).then_inc(kept_landed, 16)
                    sp.dma_start(v_tok[:, 0:NT, :].rearrange("p t c -> p (t c)"), kept[:, 1, :]).then_inc(kept_landed, 16)

            def load_wo0(p, i):
                sp.wait_ge(wo_done, i * NT + (NT * PAIRS * p + CREDIT))
                sp.dma_start(wo[:], wo0[:, bass.ds(i, 1), :].squeeze(1)).then_inc(wo_landed[0], 16)

            def load_pair1(p, i, lo):
                j = lo // GROUP
                if lo in (0, GROUP):
                    sp.wait_ge(kv_done, 2 * (KV_PAIRS * (p % 2) + j) + CREDIT)
                    sp.dma_start(w_k[:], w2[:, :, D + j * P:D + (j + 1) * P]).then_inc(wkv_landed, 16)
                    sp.dma_start(w_v[:], w2[:, :, D + (KV_PAIRS + j) * P:D + (KV_PAIRS + j + 1) * P]).then_inc(wkv_landed, 16)
                sp.wait_ge(q_done, i + (PAIRS * (p % 2) + CREDIT))
                for a in range(2):
                    col = (2 * GROUP * j + GROUP * a - GROUP * j) * DH
                    sp.dma_start(w_q[:, :, a * DH:(a + 1) * DH], w2[:, :, bass.ds(i * DH + col, DH)]).then_inc(wq_landed, 16)

            def load_wo1(p, i, lo):
                j = lo // GROUP
                sp.wait_ge(wo_done, i * NT + (NT * PAIRS * p + CREDIT))
                for a in range(2):
                    sp.dma_start(wo[a * DH:(a + 1) * DH, :],
                                 wo1[a][:, j, bass.ds(i - GROUP * j, 1), :].squeeze(1)).then_inc(wo_landed[1], 16)

            for t in range(TT):
                sp.dma_start(h[:, t, :], x_tiles[t]).then_inc(x_landed, 16)
            sp.dma_start(gain_b[:, 0, :], sb_norm[0:1, :].broadcast_to([P, D])).then_inc(attn_gain_landed, 16)
            with sp.Fori(0, PAIRS) as i:
                load_pair0(0, i)
                load_wo0(0, i)
                sp.wait_ge(proj_copied, i * 3 + 3)
                kept = kv_kept[bass.ds(i, 1)].squeeze(0)
                sp.dma_start(kept[:, 0, :], kT[:, 0:NS]).then_inc(kv_stored, 16)
                sp.dma_start(kept[:, 1, :], v_tok[:, 0:NT, :].rearrange("p t c -> p (t c)")).then_inc(kv_stored, 16)
            sp.wait_ge(kv_stored, 32 * PAIRS + CREDIT)
            sp.dma_start(gain_b[:, 1, :], ffn_norm[0:1, :].broadcast_to([P, D])).then_inc(peer_gain_landed, 16)
            sp.dma_start(qk_gain[:, 0, :], sw_q_gain[0:1, :].broadcast_to([P, DH])).then_inc(small_landed, 16)
            sp.dma_start(qk_gain[:, 1, :], sw_k_gain[0:1, :].broadcast_to([P, DH])).then_inc(small_landed, 16)
            sp.dma_start(sink_b[:], sw_sinks[0:1, :].broadcast_to([P, SW_HEADS])).then_inc(small_landed, 16)
            load_peer(0, 0)
            for s in range(STAGES):
                p = s + 1
                if p == 2:
                    sp.wait_ge(proj_done, 3 * PAIRS * 2 + CREDIT)

                def iteration(hd, first, last, lo):
                    if p == 1:
                        load_pair0(p, hd)
                    elif p < STAGES:
                        load_pair1(p, hd, lo)
                    if not last:
                        load_peer(s, hd + 1)
                    elif p < STAGES:
                        load_peer(s + 1, 0)
                    if p == 1:
                        load_wo0(p, hd)
                    elif p < STAGES:
                        load_wo1(p, hd, lo)
                    if first and s == 0:
                        sp.wait_ge(xn_ready, 3 * NT)
                        sp.dma_start(gain_b[:, 0, :], sw_norm[0:1, :].broadcast_to([P, D])).then_inc(attn_gain_landed, 16)
                    if first and s == 1:
                        sp.wait_ge(xn_ready, 4 * NT)
                        sp.dma_start(gain_b[:, 1, :], ffn_norm[1:2, :].broadcast_to([P, D])).then_inc(peer_gain_landed, 16)

                run(sp, s, iteration)
                if s >= 2:
                    sp.wait_ge(acc_added, UNITS * (s + 1))
                    for t in range(first_tile(s), first_tile(s) + NT):
                        sp.dma_start(out_tiles[t], h[:, t, :]).then_inc(out_stored, 16)
            sp.wait_ge(out_stored, 16 * TT)

        @block.gpsimd
        def _(pool):
            pool.memset(eps[:], RMS_EPS).then_inc(const_ready, 1)
            pool.memset(ident[:], 0.0).then_inc(pool_step, 1)
            pool.memset(ident_bf[:], 0.0).then_inc(pool_step, 1)
            pool.memset(later_bf[:], MASKED).then_inc(pool_step, 1)
            pool.iota(dist[:], pattern=[[-1, WIN]], base=P, channel_multiplier=1,
                      allow_small_or_imprecise_dtypes=True).then_inc(pool_step, 1)
            pool.wait_ge(pool_step, 4)
            for m in (ident, ident_bf):
                pool.affine_select(out=m[:], in_=m[:], compare_op=ALU.not_equal, fill=1.0, base=0,
                                   pattern=[[-1, P]], channel_multiplier=1).then_inc(const_ready, 1)
            pool.affine_select(out=later_bf[:], in_=later_bf[:], compare_op=ALU.is_ge, fill=0.0, base=0,
                               pattern=[[1, P]], channel_multiplier=-1).then_inc(const_ready, 1)
            pool.affine_select(out=dist[:], in_=dist[:], compare_op=ALU.is_ge, fill=-MASKED, base=P,
                               pattern=[[-1, WIN]], channel_multiplier=1).then_inc(pool_step, 1)
            pool.wait_ge(pool_step, 5)
            pool.affine_select(out=dist[:], in_=dist[:], compare_op=ALU.is_gt, fill=-MASKED, base=0,
                               pattern=[[1, WIN]], channel_multiplier=-1).then_inc(const_ready, 1)
            pool.iota(slot_no[:], pattern=[[1, TOPK]], base=0, channel_multiplier=0,
                      allow_small_or_imprecise_dtypes=True).then_inc(const_ready, 1)
            for hd in range(SW_HEADS):
                pool.memset(neg_slope[:, hd:hd + 1], -2.0 ** (-8.0 * (hd + 1) / SW_HEADS)).then_inc(const_ready, 1)

            for s in range(STAGES):
                with pool.Fori(0, PEER_HEADS) as hd:
                    for t in range(NT):
                        first = UNITS * s + t
                        pool.wait_ge(expert_ready, hd * NT + (first + 1))
                        pool.sem_inc(gathers_issued, 1)
                        for table, ring, landed, free in ((peer_u, u_ring, u_landed, u_slots_free),
                                                          (peer_v, v_ring, v_landed, v_slots_free)):
                            for k in range(TOPK):
                                pool.wait_ge(free, hd * (NT * TOPK) + (first * TOPK + k + 1))
                                pool.sem_inc(gathers_issued, 1)
                                pool.indirect_dma_start(
                                    ring[:, k % SLOTS, :], None, table.rearrange("l e d -> (l e) d"),
                                    bass.IndirectOffsetOnAxis(ap=expert[:, t, k:k + 1], axis=0),
                                    element_offset=(s // 2) * KEYS * KEYS * D).then_inc(landed[k % SLOTS], 16)

        CONSTS = 6 + SW_HEADS

        @block.scalar
        def _(act):
            def norm(m, s, xT):
                for n in range(NT):
                    act.activation(xn[:, first_tile(s) + n, :], h[:, first_tile(s) + n, :], ACT.Square,
                                   accum_out=sumsq[:, n:n + 1]).then_inc(sumsq_ready, 1)
                act.wait_ge(sumsq_ready, NT * (m + 1))
                act.activation(root[:], sumsq[:], ACT.Sqrt, bias=eps[:], scale=1.0 / D).then_inc(root_ready, 1)
                for n in range(NT):
                    for b, bank in enumerate((z_own, t_own)):
                        act.wait_ge(xT_done, 2 * (NT * m + n) + b + 1)
                        act.activation(xT[:, 4 * b:4 * b + 4, n * P:(n + 1) * P],
                                       bank[:].rearrange("p (k s) -> p k s", k=4), ACT.Copy).then_inc(xT_ready, 1)

            def copy_proj0(p, i):
                lo = first_tile(p)
                act.wait_ge(proj_done, i * 3 + (24 * p + 2 + CREDIT))
                act.activation(qT[:], qk_bank[:, 0:NS], ACT.Copy).then_inc(proj_copied, 1)
                if p == 0:
                    act.wait_ge(kv_stored, i * 32 + CREDIT)
                act.activation(kT[:, lo * P:lo * P + NS], qk_bank[:, NS:2 * NS], ACT.Copy).then_inc(proj_copied, 1)
                act.wait_ge(proj_done, i * 3 + (24 * p + 3 + CREDIT))
                act.activation(v_tok[:, lo:lo + NT, :].rearrange("p t c -> p (t c)"), vo_bank[:, 0:NS],
                               ACT.Copy).then_inc(proj_copied, 1)

            def gates0(p, i, u):
                w = (first_tile(p) + u % NT + 1) * P
                z = z_banks[p][u % 2]
                act.wait_ge(z_done, i * STEPS + (STEPS * PAIRS * p + u + 1))
                if u >= 2:
                    act.wait_ge(attn_ready, i * STEPS + (STEPS * PAIRS * p + u - 1))
                act.activation(fail[:, u % 2, 0:w], z[:, 0:w], ACT.Sigmoid, scale=-SCALE)
                act.activation(take[:, u % 2, 0:w], z[:, 0:w], ACT.Sigmoid, scale=SCALE).then_inc(gates_ready, 1)

            def copy_attnT0(p, i, u):
                w = (first_tile(p) + u % NT + 1) * P
                act.wait_ge(attnT_done, i * STEPS + (STEPS * PAIRS * p + u + 1))
                act.activation(attnT[:, u % 2, 0:w], t_banks[p][u % 2][:, 0:w], ACT.Copy).then_inc(attnT_ready, 1)

            def copy_o0(p, i, a):
                rows = slice(a * DH, (a + 1) * DH)
                act.wait_ge(o_done, i * STEPS + (STEPS * PAIRS * p + NT * (a + 1)))
                act.activation(oT[rows, :], o_part[rows, :], ACT.Copy).then_inc(oT_ready, 1)

            def copy_proj1(p, i, lo):
                j = lo // GROUP
                if lo in (0, GROUP):
                    if p % 2:
                        act.activation(kT_win[:, j, 0:P], kT_win[:, j, NT * P:(NT + 1) * P], ACT.Copy).then_inc(kept_copied, 1)
                        act.activation(v_win[:, j, 0, :], v_win[:, j, NT, :], ACT.Copy).then_inc(kept_copied, 1)
                        act.wait_ge(kept_copied, 2 * (j + 1))
                    act.wait_ge(kv_done, 2 * (KV_PAIRS * (p % 2) + j + 1) + CREDIT)
                    act.activation(v_win[:, j, 1:NT + 1, :].rearrange("p t c -> p (t c)"), vo_bank[:, 0:NS],
                                   ACT.Copy).then_inc(v_copied, 1)
                w = 2 * NS if lo in (0, GROUP) else NS
                act.wait_ge(q_done, i + (PAIRS * (p % 2) + 1 + CREDIT))
                act.activation(head_tok[:, 0:w], qk_bank[:, 0:w], ACT.Copy)
                act.activation(head_sq[:, 0:w], qk_bank[:, 0:w], ACT.Square).then_inc(q_copied, 1)

            def root1(p, i, lo):
                n = 4 * NT if lo in (0, GROUP) else 2 * NT
                act.wait_ge(headss_ready, i + (PAIRS * (p % 2) + 1))
                act.activation(head_root[:, 0:n], head_ss[:, 0:n], ACT.Sqrt, bias=eps[:],
                               scale=1.0 / DH).then_inc(headroot_ready, 1)

            def copy_headT1(p, i, lo):
                j = lo // GROUP
                act.wait_ge(headT_done, i + (PAIRS * (p % 2) + 1))
                if lo in (0, GROUP):
                    act.activation(kT_win[:, j, P:(NT + 1) * P], t_own[:, NS:2 * NS], ACT.Copy)
                act.activation(qT[:], t_own[:, 0:NS], ACT.Copy).then_inc(headT_ready, 1)

            def exp1(p, i, a):
                act.wait_ge(negtop_ready, i * 2 + (2 * PAIRS * (p % 2) + a + 1))
                for n in range(NT):
                    c = P if p % 2 == 0 and n == 0 else 0
                    act.activation(prob[:, a, n, c:WIN], sw_score[:, a, n, c:WIN], ACT.Exp,
                                   bias=neg_top[:, a, n:n + 1], accum_out=row_sum[:, a, n:n + 1])
                act.activation(sink_exp[:, a, :], sink_arg[:, a, :], ACT.Exp).then_inc(exp_ready, 1)

            def copy_probT1(p, i, a):
                act.wait_ge(probT_done, i * 2 + (2 * PAIRS * (p % 2) + a + 1))
                w0 = P if p % 2 == 0 else 0
                act.activation(attnT[:, a, w0:2 * WIN], t_own[:, w0:2 * WIN], ACT.Copy).then_inc(probT_ready, 1)

            def copy_o1(p, i, a):
                rows = slice(a * DH, (a + 1) * DH)
                act.wait_ge(swo_done, i * 2 + (2 * PAIRS * (p % 2) + a + 1))
                act.activation(oT[rows, :], o_part[rows, :], ACT.Copy).then_inc(swoT_ready, 1)

            def copy_scores(s, hd):
                act.wait_ge(keysT_done, hd + (s * PEER_HEADS + 1))
                act.activation(keysT[:].rearrange("p a b -> p (a b)"), vo_bank[:, 0:2 * P],
                               ACT.Copy).then_inc(keysT_ready, 1)
                act.wait_ge(pq_done, hd * 2 + (s * 2 * PEER_HEADS + 2 + CREDIT))
                act.activation(pqT[:].rearrange("p a s -> p (a s)"), qk_bank[:], ACT.Copy).then_inc(pqT_ready, 1)
                act.wait_ge(score_done, hd + (s * PEER_HEADS + 1))
                act.activation(scores[:].rearrange("p t a n -> p (t a n)"), vo_bank[:], ACT.Copy).then_inc(scores_ready, 1)

            def unit_gate(s, hd, t):
                act.wait_ge(best_ready, hd * NT + (UNITS * s + t + 1))
                act.activation(gate[:], cand_top[:], ACT.Exp, bias=neg_best[:],
                               accum_out=gate_sum[:]).then_inc(gate_ready, 1)

            def unit_diag(s, hd, t):
                n = hd * NT + (UNITS * s + t + 1)
                act.wait_ge(gelu_arg_ready, n)
                act.activation(gelu_exp[:], g3[:], ACT.Exp).then_inc(gelu_exp_ready, 1)
                act.wait_ge(coef_ready, n)
                act.wait_ge(v_slots_free, hd * (NT * TOPK) + ((UNITS * s + t) * TOPK + SLOTS))
                for k in range(TOPK):
                    act.activation(diag[:, k, :], ident[:], ACT.Copy, scale=coef[:, k:k + 1]).then_inc(diag_ready, 1)

            act.sem_inc(kv_stored, CREDIT)
            act.wait_ge(const_ready, CONSTS)
            act.wait_ge(x_landed, 16 * TT)
            norm(0, 0, attn_xT)
            with act.Fori(0, PAIRS) as i:
                copy_proj0(0, i)
                gates0(0, i, 0)
                gates0(0, i, 1)
                copy_attnT0(0, i, 0)
                gates0(0, i, 2)
                copy_attnT0(0, i, 1)
                gates0(0, i, 3)
                copy_o0(0, i, 0)
                copy_attnT0(0, i, 2)
                copy_attnT0(0, i, 3)
                copy_o0(0, i, 1)
            for s in range(STAGES):
                p = s + 1
                act.wait_ge(h_added, NT * PAIRS * p)
                norm(2 * s + 1, s, peer_xT)
                copy_scores(s, 0)
                if p < STAGES:
                    if s:
                        act.wait_ge(acc_added, UNITS * s)
                    norm(2 * s + 2, p, attn_xT)

                def iteration(hd, first, last, lo):
                    unit_gate(s, hd, 0)
                    if p == 1:
                        copy_proj0(p, hd)
                    elif p < STAGES:
                        copy_proj1(p, hd, lo)
                    unit_diag(s, hd, 0)
                    if p == 1:
                        gates0(p, hd, 0)
                        gates0(p, hd, 1)
                        copy_attnT0(p, hd, 0)
                        copy_attnT0(p, hd, 1)
                        copy_o0(p, hd, 0)
                    elif p < STAGES:
                        root1(p, hd, lo)
                        copy_headT1(p, hd, lo)
                    unit_gate(s, hd, 1)
                    if not last:
                        copy_scores(s, hd + 1)
                    unit_diag(s, hd, 1)
                    if p == 1:
                        gates0(p, hd, 2)
                        gates0(p, hd, 3)
                        copy_attnT0(p, hd, 2)
                        copy_attnT0(p, hd, 3)
                        copy_o0(p, hd, 1)
                    elif p < STAGES:
                        exp1(p, hd, 0)
                        exp1(p, hd, 1)
                        copy_probT1(p, hd, 0)
                        copy_o1(p, hd, 0)
                        copy_probT1(p, hd, 1)
                        copy_o1(p, hd, 1)

                run(act, s, iteration)

        @block.tensor
        def _(pe):
            def norm(m, s):
                for n in range(NT):
                    pe.wait_ge(xn_ready, NT * m + n + 1)
                    for b, bank in enumerate((z_own, t_own)):
                        if n >= 1:
                            pe.wait_ge(xT_ready, 2 * (NT * m + n - 1) + b + 1)
                        for k in range(4):
                            ins = pe.transpose(bank[:, k * P:(k + 1) * P],
                                               xn[:, first_tile(s) + n, (4 * b + k) * P:(4 * b + k + 1) * P], ident[:])
                        ins.then_inc(xT_done, 1)

            def project_T(dst, w, xT):
                for k in range(KC):
                    ins = pe.matmul(dst, w[:, k, :], xT[:, k, :], start=(k == 0), stop=(k == KC - 1))
                return ins

            def project(dst, w, xT):
                for n in range(NT):
                    for k in range(KC):
                        ins = pe.matmul(dst[:, n * P:(n + 1) * P], xT[:, k, n * P:(n + 1) * P], w[:, k, :],
                                        start=(k == 0), stop=(k == KC - 1))
                return ins

            def output(p, i, n, banks):
                layer = p // 2
                if n == 0:
                    ready, before = (oT_ready, 2 * PAIRS * p) if layer == 0 else (swoT_ready, 2 * PAIRS * (p % 2))
                    pe.wait_ge(wo_landed[layer], i * (16 + 16 * layer) + (16 + 16 * layer) * (PAIRS * (p % 2) + 1))
                    pe.wait_ge(ready, i * 2 + (before + 2))
                for c in range(HALVES):
                    ins = pe.matmul(banks[c], oT[:, n * P:(n + 1) * P], wo[:, c * BANK:(c + 1) * BANK],
                                    start=True, stop=True)
                ins.then_inc(wo_done, 1)

            def project0(p, i):
                pe.wait_ge(wqkv_landed, i * 48 + 48 * (PAIRS * p + 1))
                project_T(qk_bank[:, 0:NS], w_q, attn_xT).then_inc(proj_done, 1)
                project_T(qk_bank[:, NS:2 * NS], w_k, attn_xT).then_inc(proj_done, 1)
                project(vo_bank, w_v, attn_xT).then_inc(proj_done, 1)

            def z0(p, i, u):
                a, n = u // NT, u % NT
                rows = slice(a * DH, (a + 1) * DH)
                t = first_tile(p) + n
                z = z_banks[p][u % 2]
                if u == 0:
                    pe.wait_ge(proj_copied, i * 3 + (24 * p + 3))
                    if p:
                        pe.wait_ge(kept_landed, i * 32 + 32)
                lag = 2 if p == 0 else 1
                if u >= lag:
                    pe.wait_ge(gates_ready, i * STEPS + (STEPS * PAIRS * p + u + 1 - lag))
                pe.matmul(z[:, 0:(t + 1) * P], qT[rows, n * P:(n + 1) * P], kT[rows, 0:(t + 1) * P],
                          start=True, stop=False, skip_group_check=True)
                pe.matmul(z[:, t * P:(t + 1) * P], ident_bf[:], later_bf[:],
                          start=False, stop=True, skip_group_check=True).then_inc(z_done, 1)

            def transpose0(p, i, u):
                t = first_tile(p) + u % NT
                pe.wait_ge(attn_ready, i * STEPS + (STEPS * PAIRS * p + u + 1))
                for kb in range(t + 1):
                    ins = pe.transpose(t_banks[p][u % 2][:, kb * P:(kb + 1) * P],
                                       attn[:, u % 2, kb * P:(kb + 1) * P], ident[:])
                ins.then_inc(attnT_done, 1)

            def apply0(p, i, u):
                a, n = u // NT, u % NT
                rows = slice(a * DH, (a + 1) * DH)
                t = first_tile(p) + n
                pe.wait_ge(attnT_ready, i * STEPS + (STEPS * PAIRS * p + u + 1))
                for kb in range(t + 1):
                    ins = pe.matmul(o_part[rows, n * P:(n + 1) * P], v_tok[:, kb, rows],
                                    attnT[:, u % 2, kb * P:(kb + 1) * P], start=(kb == 0), stop=(kb == t))
                ins.then_inc(o_done, 1)

            def project1(p, i, lo):
                j = lo // GROUP
                if lo in (0, GROUP):
                    pe.wait_ge(wkv_landed, 32 * (KV_PAIRS * (p % 2) + j + 1))
                    project(qk_bank[:, NS:2 * NS], w_k, attn_xT).then_inc(kv_done, 1)
                    project(vo_bank, w_v, attn_xT).then_inc(kv_done, 1)
                pe.wait_ge(wq_landed, i * 32 + 32 * (PAIRS * (p % 2) + 1))
                project(qk_bank, w_q, attn_xT).then_inc(q_done, 1)

            def transpose_heads1(p, i, lo):
                pe.wait_ge(headn_ready, i + (PAIRS * (p % 2) + 1))
                for n in range(2 * NT if lo in (0, GROUP) else NT):
                    ins = pe.transpose(t_own[:, n * P:(n + 1) * P], head_tok[:, n * P:(n + 1) * P], ident[:])
                ins.then_inc(headT_done, 1)

            def z1(p, i, a, lo):
                j = lo // GROUP
                rows = slice(a * DH, (a + 1) * DH)
                if a == 0:
                    pe.wait_ge(headT_ready, i + (PAIRS * (p % 2) + 1))
                else:
                    pe.wait_ge(swz_read, i * 2 + (2 * PAIRS * (p % 2) + 1))
                for n in range(NT):
                    c = P if p % 2 == 0 and n == 0 else 0
                    ins = pe.matmul(z_own[:, n * WIN + c:(n + 1) * WIN], qT[rows, n * P:(n + 1) * P],
                                    kT_win[rows, j, n * P + c:n * P + WIN], start=True, stop=True)
                ins.then_inc(swz_done, 1)

            def transpose1(p, i, a):
                pe.wait_ge(prob_ready, i * 2 + (2 * PAIRS * (p % 2) + a + 1))
                if a:
                    pe.wait_ge(probT_ready, i * 2 + (2 * PAIRS * (p % 2) + a))
                for n in range(NT):
                    for b in range(2):
                        if p % 2 == 0 and n == 0 and b == 0:
                            continue
                        ins = pe.transpose(t_own[:, n * WIN + b * P:n * WIN + (b + 1) * P],
                                           prob[:, a, n, b * P:(b + 1) * P], ident[:])
                ins.then_inc(probT_done, 1)

            def apply1(p, i, a, lo):
                j = lo // GROUP
                rows = slice(a * DH, (a + 1) * DH)
                pe.wait_ge(probT_ready, i * 2 + (2 * PAIRS * (p % 2) + a + 1))
                for n in range(NT):
                    blocks = [1] if p % 2 == 0 and n == 0 else [0, 1]
                    for b in blocks:
                        ins = pe.matmul(o_part[rows, n * P:(n + 1) * P], v_win[:, j, n + b, rows],
                                        attnT[:, a, n * WIN + b * P:n * WIN + (b + 1) * P],
                                        start=(b == blocks[0]), stop=(b == 1))
                ins.then_inc(swo_done, 1)

            def score_head(s, hd):
                pe.wait_ge(wpq_landed, hd * 32 + 32 * (s * PEER_HEADS + 1))
                for half in range(2):
                    ins = pe.transpose(vo_bank[:, half * P:(half + 1) * P], keys[:, half, :], ident[:])
                ins.then_inc(keysT_done, 1)
                for half in range(2):
                    project_T(qk_bank[:, half * NS:(half + 1) * NS], w_pq[:, :, half * P:(half + 1) * P],
                              peer_xT).then_inc(pq_done, 1)
                pe.wait_ge(keysT_ready, hd + (s * PEER_HEADS + 1))
                pe.wait_ge(pqT_ready, hd + (s * PEER_HEADS + 1))
                for t in range(NT):
                    for half in range(2):
                        ins = pe.matmul(vo_bank[:, (2 * t + half) * P:(2 * t + half + 1) * P],
                                        pqT[:, half, t * P:(t + 1) * P], keysT[:, half, :], start=True, stop=True)
                ins.then_inc(score_done, 1)

            def unit(s, hd, t, between):
                n = UNITS * s + t
                if not (isinstance(hd, int) and n + hd * NT == 0):
                    pe.wait_ge(acc_added, hd * NT + n)
                for k in range(TOPK):
                    pe.wait_ge(v_landed[k % SLOTS], hd * (NT * 32) + (n * 32 + 16 * (k // SLOTS + 1)))
                    pe.wait_ge(diag_ready, hd * (NT * TOPK) + (n * TOPK + k + 1))
                    for c in range(HALVES):
                        ins = pe.matmul(acc[c][:], diag[:, k, :], v_ring[:, k % SLOTS, c * BANK:(c + 1) * BANK],
                                        start=(k == 0), stop=(k == TOPK - 1), skip_group_check=True)
                    ins.then_inc(v_slots_free, 1)
                    for work_piece in between.get(k, ()):
                        work_piece()

            pe.sem_inc(v_slots_free, SLOTS)
            for c in (proj_done, q_done, kv_done, pq_done, wo_done):
                pe.sem_inc(c, CREDIT)
            pe.wait_ge(const_ready, CONSTS)
            norm(0, 0)
            pe.wait_ge(xT_ready, 2 * NT)
            with pe.Fori(0, PAIRS) as i:
                project0(0, i)
                z0(0, i, 0)
                z0(0, i, 1)
                transpose0(0, i, 0)
                z0(0, i, 2)
                apply0(0, i, 0)
                transpose0(0, i, 1)
                z0(0, i, 3)
                apply0(0, i, 1)
                transpose0(0, i, 2)
                apply0(0, i, 2)
                transpose0(0, i, 3)
                apply0(0, i, 3)
                output(0, i, 0, [z_own[:], t_own[:]])
                output(0, i, 1, [x_cur[:, 0:BANK], x_cur[:, BANK:D]])
                pe.wait_ge(h_added, i * NT + NT)
            for s in range(STAGES):
                p = s + 1
                norm(2 * s + 1, s)
                pe.wait_ge(xT_ready, 2 * NT * (2 * s + 2))
                score_head(s, 0)
                if p < STAGES:
                    norm(2 * s + 2, p)
                    pe.wait_ge(xT_ready, 2 * NT * (2 * s + 3))
                pe.wait_ge(scores_ready, s * PEER_HEADS + 1)

                def iteration(hd, first, last, lo):
                    if p < STAGES and not first:
                        output(p, hd - 1, 0, [z_own[:], t_own[:]])
                    if p == 1:
                        project0(p, hd)
                        pe.wait_ge(proj_copied, hd * 3 + (24 * p + 3))
                    elif p < STAGES:
                        project1(p, hd, lo)
                        pe.wait_ge(q_copied, hd + (PAIRS * (p % 2) + 1))
                    if p < STAGES and not first:
                        output(p, hd - 1, 1, [qk_bank[:], vo_bank[:]])
                    if p < STAGES:
                        banks_read = [] if first else [lambda: pe.wait_ge(h_added, hd * NT + NT * PAIRS * p)]
                    if p == 1:
                        unit(s, hd, 0, {0: banks_read + [lambda: z0(p, hd, 0)], 2: [lambda: z0(p, hd, 1)],
                                        8: [lambda: transpose0(p, hd, 0)], 10: [lambda: apply0(p, hd, 0)],
                                        11: [lambda: transpose0(p, hd, 1)], 13: [lambda: apply0(p, hd, 1)]})
                    elif p < STAGES:
                        unit(s, hd, 0, {9: banks_read + [lambda: transpose_heads1(p, hd, lo)],
                                        13: [lambda: z1(p, hd, 0, lo)]})
                    else:
                        unit(s, hd, 0, {})
                    if not last:
                        if p == 1:
                            pe.wait_ge(oT_ready, hd * 2 + (2 * PAIRS * p + 1))
                        score_head(s, hd + 1)
                        pe.wait_ge(scores_ready, hd + (s * PEER_HEADS + 2))
                    if p == 1:
                        unit(s, hd, 1, {0: [lambda: z0(p, hd, 2)], 2: [lambda: z0(p, hd, 3)],
                                        8: [lambda: transpose0(p, hd, 2)], 10: [lambda: apply0(p, hd, 2)],
                                        11: [lambda: transpose0(p, hd, 3)], 13: [lambda: apply0(p, hd, 3)]})
                    elif p < STAGES:
                        unit(s, hd, 1, {2: [lambda: z1(p, hd, 1, lo)],
                                        9: [lambda: transpose1(p, hd, 0)], 11: [lambda: apply1(p, hd, 0, lo)],
                                        12: [lambda: transpose1(p, hd, 1)], 15: [lambda: apply1(p, hd, 1, lo)]})
                    else:
                        unit(s, hd, 1, {})

                run(pe, s, iteration)
                if p < STAGES:
                    output(p, PAIRS - 1, 0, [z_own[:], t_own[:]])
                    output(p, PAIRS - 1, 1, [qk_bank[:], vo_bank[:]])
                    pe.wait_ge(h_added, NT * PAIRS * (p + 1))

        @block.vector
        def _(dve):
            def norm(m, s, which, landed, n_landed):
                dve.wait_ge(root_ready, m + 1)
                dve.sem_clear(dve_step)
                dve.reciprocal(rstd[:], root[:]).then_inc(dve_step, 1)
                dve.wait_ge(dve_step, 1)
                dve.wait_ge(landed, n_landed)
                for n in range(NT):
                    t = first_tile(s) + n
                    dve.scalar_tensor_tensor(out=xn[:, t, :], in0=h[:, t, :], scalar=rstd[:, n:n + 1],
                                             in1=gain_b[:, which, :], op0=ALU.mult, op1=ALU.mult).then_inc(xn_ready, 1)

            def add_output(p, i, n, banks):
                dve.wait_ge(wo_done, i * NT + (NT * PAIRS * p + n + 1 + CREDIT))
                t = first_tile(p) + n
                for c in range(HALVES):
                    part = h[:, t, c * BANK:(c + 1) * BANK]
                    ins = dve.tensor_tensor(part, banks[c], part, ALU.add)
                ins.then_inc(h_added, 1)

            def stick0(p, i, u):
                w = (first_tile(p) + u % NT + 1) * P
                n = STEPS * PAIRS * p + u
                dve.wait_ge(gates_ready, i * STEPS + (n + 1))
                dve.tensor_tensor_scan(left[:, u % 2, BANK - w:BANK][:, ::-1], fail[:, u % 2, 0:w][:, ::-1],
                                       fail[:, u % 2, 0:w][:, ::-1], 1.0, ALU.mult, ALU.bypass).then_inc(left_ready, 1)
                if u >= 2:
                    dve.wait_ge(attnT_done, i * STEPS + (n - 1))
                dve.wait_ge(left_ready, i * STEPS + (n + 1))
                dve.tensor_tensor(attn[:, u % 2, 0:w], take[:, u % 2, 0:w], left[:, u % 2, BANK + 1 - w:BANK + 1],
                                  ALU.mult).then_inc(attn_ready, 1)

            def head_sums1(p, i, lo):
                w = 2 * NS if lo in (0, GROUP) else NS
                dve.wait_ge(q_copied, i + (PAIRS * (p % 2) + 1))
                dve.tensor_reduce(head_ss[:, 0:w // DH], head_sq[:, 0:w].rearrange("p (n c) -> p n c", c=DH), AX_X,
                                  ALU.add).then_inc(headss_ready, 1)

            def head_norm1(p, i, lo):
                w = 2 * NS if lo in (0, GROUP) else NS
                tok = head_tok[:, 0:w].rearrange("p (n c) -> p n c", c=DH)
                n, q = w // DH, NS // DH
                dve.sem_clear(dve_step)
                dve.wait_ge(headroot_ready, i + (PAIRS * (p % 2) + 1))
                dve.reciprocal(head_rstd[:, 0:n], head_root[:, 0:n]).then_inc(dve_step, 1)
                dve.wait_ge(dve_step, 1)
                dve.tensor_tensor(tok, tok, spread(head_rstd[:, 0:n], 2, [P, n, DH]), ALU.mult).then_inc(dve_step, 1)
                dve.wait_ge(dve_step, 2)
                if n > q:
                    dve.tensor_tensor(tok[:, q:n, :], tok[:, q:n, :], spread(qk_gain[:, 1, :], 1, [P, n - q, DH]), ALU.mult)
                dve.tensor_tensor(tok[:, 0:q, :], tok[:, 0:q, :], spread(qk_gain[:, 0, :], 1, [P, q, DH]),
                                  ALU.mult).then_inc(headn_ready, 1)

            def biased1(p, i, a, lo):
                j = lo // GROUP
                hd = i + (GROUP * j + GROUP * a)
                slope, sink = neg_slope[:, bass.ds(hd, 1)], sink_b[:, bass.ds(hd, 1)]
                z = z_own[:].rearrange("p (n w) -> p n w", n=NT)
                base = 2 * PAIRS * (p % 2) + a + 1
                dve.sem_clear(dve_step)
                dve.wait_ge(swz_done, i * 2 + base)
                if p % 2 == 0:
                    dve.scalar_tensor_tensor(out=sw_score[:, a, 0, P:WIN], in0=dist[:, P:WIN], scalar=slope,
                                             in1=z[:, 0, P:WIN], op0=ALU.mult, op1=ALU.add)
                    dve.scalar_tensor_tensor(out=sw_score[:, a, 1, :], in0=dist[:], scalar=slope,
                                             in1=z[:, 1, :], op0=ALU.mult, op1=ALU.add).then_inc(swz_read, 1)
                else:
                    dve.scalar_tensor_tensor(out=sw_score[:, a, :, :], in0=spread(dist[:], 1, [P, NT, WIN]), scalar=slope,
                                             in1=z, op0=ALU.mult, op1=ALU.add).then_inc(swz_read, 1)
                dve.wait_ge(swz_read, i * 2 + base)
                dve.tensor_reduce(top[:, a, :], sw_score[:, a, :, :], AX_X, ALU.max).then_inc(dve_step, 1)
                dve.wait_ge(dve_step, 1)
                dve.tensor_scalar(neg_top[:, a, :], top[:, a, :], sink, -1.0, ALU.max, ALU.mult).then_inc(dve_step, 1)
                dve.wait_ge(dve_step, 2)
                dve.tensor_scalar(sink_arg[:, a, :], neg_top[:, a, :], sink, None, ALU.add).then_inc(negtop_ready, 1)

            def normalise1(p, i, a):
                dve.sem_clear(dve_step)
                dve.wait_ge(exp_ready, i * 2 + (2 * PAIRS * (p % 2) + a + 1))
                dve.tensor_tensor(denom[:, a, :], row_sum[:, a, :], sink_exp[:, a, :], ALU.add).then_inc(dve_step, 1)
                dve.wait_ge(dve_step, 1)
                dve.reciprocal(inv_denom[:, a, :], denom[:, a, :]).then_inc(dve_step, 1)
                dve.wait_ge(dve_step, 2)
                dve.tensor_tensor(prob[:, a, :, :], prob[:, a, :, :], spread(inv_denom[:, a, :], 2, [P, NT, WIN]),
                                  ALU.mult).then_inc(prob_ready, 1)

            def top16(values, others, top_out, idx_out, step):
                step(dve.max(top_out[:, 0:TOP8], values))
                step(dve.match_replace(others, top_out[:, 0:TOP8], values, LOWEST))
                step(dve.max(top_out[:, TOP8:TOPK], others))
                dve.max_index(idx_out[:, 0:TOP8], top_out[:, 0:TOP8], values)
                step(dve.max_index(idx_out[:, TOP8:TOPK], top_out[:, TOP8:TOPK], others))

            def choose(s, hd, t):
                dve.sem_clear(dve_step)
                count = [0]

                def step(ins):
                    count[0] += 1
                    ins.then_inc(dve_step, 1)
                    dve.wait_ge(dve_step, count[0])

                if t == 0:
                    dve.wait_ge(scores_ready, hd + (s * PEER_HEADS + 1))
                    dve.sem_inc(dve_step, 1)
                    count[0] = 1
                for half in range(2):
                    top16(scores[:, t, half, :], rest[:, half, :], half_top[:, half, :], half_idx[:, half, :], step)
                step(dve.tensor_tensor(cand[:], spread(half_top[:, 0, :], 2, [P, TOPK, TOPK]),
                                       spread(half_top[:, 1, :], 1, [P, TOPK, TOPK]), ALU.add))
                top16(cand[:].rearrange("p a b -> p (a b)"), cand_rest[:], cand_top[:], cand_idx[:], step)
                dve.tensor_scalar(neg_best[:], cand_top[:, 0:1], -1.0, None, ALU.mult).then_inc(best_ready, 1)
                dve.tensor_copy(half_idx_f[:], half_idx[:])
                dve.tensor_single_scalar(place[:, 0, :], cand_idx[:], 4, ALU.logical_shift_right)
                step(dve.tensor_single_scalar(place[:, 1, :], cand_idx[:], TOPK - 1, ALU.bitwise_and))
                step(dve.tensor_copy(place_f[:], place[:]))
                shape = [P, 2, TOPK, TOPK]
                step(dve.tensor_tensor(onehot[:], spread(place_f[:], 3, shape),
                                       slot_no[:].unsqueeze(1).unsqueeze(1).broadcast_to(shape), ALU.is_equal))
                step(dve.tensor_tensor(onehot[:], onehot[:], spread(half_idx_f[:], 2, shape), ALU.mult))
                step(dve.tensor_reduce(picked[:], onehot[:], AX_X, ALU.add))
                n = UNITS * s + t
                if not (isinstance(hd, int) and n + hd * NT < 2):
                    dve.wait_ge(v_slots_free, hd * (NT * TOPK) + ((n - 1) * TOPK + SLOTS))
                dve.scalar_tensor_tensor(out=expert[:, t, :], in0=picked[:, 0, :], scalar=float(KEYS),
                                         in1=picked[:, 1, :], op0=ALU.mult, op1=ALU.add).then_inc(expert_ready, 1)

            def products(s, hd, t, between):
                n = UNITS * s + t
                dve.sem_clear(dve_step)
                dve.tensor_copy(x_cur[:], xn[:, first_tile(s) + t, :]).then_inc(dve_step, 1)
                dve.wait_ge(dve_step, 1)
                for k in range(TOPK):
                    dve.wait_ge(u_landed[k % SLOTS], hd * (NT * 32) + (n * 32 + 16 * (k // SLOTS + 1)))
                    row = u_ring[:, k % SLOTS, :]
                    dve.tensor_tensor_reduce(row, row, x_cur[:], 1.0, 0.0, ALU.mult, ALU.add,
                                             hid[:, k:k + 1]).then_inc(u_slots_free, 1)
                    for work_piece in between.get(k, ()):
                        work_piece()

            def add_unit(s, hd, t):
                n = UNITS * s + t
                dve.wait_ge(v_slots_free, hd * (NT * TOPK) + ((n + 1) * TOPK + SLOTS))
                for c in range(HALVES):
                    part = h[:, first_tile(s) + t, c * BANK:(c + 1) * BANK]
                    ins = dve.tensor_tensor(part, acc[c][:], part, ALU.add)
                ins.then_inc(acc_added, 1)

            def coefficients(s, hd, t):
                n = UNITS * s + t
                count = [0]

                def step(ins):
                    count[0] += 1
                    ins.then_inc(dve_step, 1)
                    dve.wait_ge(dve_step, count[0])

                dve.sem_clear(dve_step)
                dve.wait_ge(u_slots_free, hd * (NT * TOPK) + ((n + 1) * TOPK + SLOTS))
                step(dve.tensor_tensor(g1[:], hid[:], hid[:], ALU.mult))
                step(dve.tensor_scalar(g2[:], g1[:], -GELU_C * GELU_A, -GELU_C, ALU.mult, ALU.add))
                dve.tensor_tensor(g3[:], g2[:], hid[:], ALU.mult).then_inc(gelu_arg_ready, 1)
                dve.wait_ge(gate_ready, hd * NT + (n + 1))
                dve.reciprocal(inv_gate[:], gate_sum[:])
                dve.wait_ge(gelu_exp_ready, hd * NT + (n + 1))
                step(dve.tensor_scalar(g1[:], gelu_exp[:], HUGE, 1.0, ALU.min, ALU.add))
                step(dve.reciprocal(g2[:], g1[:]))
                step(dve.tensor_tensor(g1[:], hid[:], g2[:], ALU.mult))
                dve.scalar_tensor_tensor(out=coef[:], in0=g1[:], scalar=inv_gate[:], in1=gate[:],
                                         op0=ALU.mult, op1=ALU.mult).then_inc(coef_ready, 1)

            dve.sem_inc(u_slots_free, SLOTS)
            dve.memset(left[:, :, BANK:BANK + 1], 1.0).then_inc(dve_set, 1)
            dve.wait_ge(dve_set, 1)
            norm(0, 0, 0, attn_gain_landed, 16)
            with dve.Fori(0, PAIRS) as i:
                for u in range(STEPS):
                    stick0(0, i, u)
                add_output(0, i, 0, [z_own[:], t_own[:]])
                add_output(0, i, 1, [x_cur[:, 0:BANK], x_cur[:, BANK:D]])
            for s in range(STAGES):
                p = s + 1
                norm(2 * s + 1, s, 1, peer_gain_landed, 16 * (s // 2 + 1))
                if s:
                    add_unit(s - 1, PEER_HEADS - 1, NT - 1)
                if p == 2:
                    dve.wait_ge(small_landed, 48)
                    dve.memset(sw_score[:, :, 0, 0:P], MASKED).then_inc(dve_set, 1)
                    dve.memset(prob[:, :, 0, 0:P], 0.0).then_inc(dve_set, 1)
                    dve.tensor_scalar(qk_gain[:, 0, :], qk_gain[:, 0, :], SCALE, None, ALU.mult).then_inc(dve_set, 1)
                    dve.wait_ge(dve_set, 4)

                def iteration(hd, first, last, lo):
                    choose(s, hd, 0)
                    if first and p < STAGES:
                        norm(2 * s + 2, p, 0, attn_gain_landed, 16 * (p // 2 + 1))
                    before = {}
                    if not first:
                        before[7] = [lambda: add_unit(s, hd - 1, NT - 1)]
                        if p < STAGES:
                            before[11] = [lambda: add_output(p, hd - 1, 0, [z_own[:], t_own[:]])]
                    products(s, hd, 0, before)
                    coefficients(s, hd, 0)
                    if p < STAGES and not first:
                        add_output(p, hd - 1, 1, [qk_bank[:], vo_bank[:]])
                    if p in (2, 3):
                        head_sums1(p, hd, lo)
                    choose(s, hd, 1)
                    if p == 1:
                        stick0(p, hd, 0)
                        stick0(p, hd, 1)
                    if p in (2, 3):
                        head_norm1(p, hd, lo)
                    products(s, hd, 1, {7: [lambda: add_unit(s, hd, 0)]})
                    coefficients(s, hd, 1)
                    if p == 1:
                        stick0(p, hd, 2)
                        stick0(p, hd, 3)
                    if p in (2, 3):
                        biased1(p, hd, 0, lo)
                        biased1(p, hd, 1, lo)
                        normalise1(p, hd, 0)
                        normalise1(p, hd, 1)

                run(dve, s, iteration)
                if p < STAGES:
                    add_output(p, PAIRS - 1, 0, [z_own[:], t_own[:]])
                    add_output(p, PAIRS - 1, 1, [qk_bank[:], vo_bank[:]])
            add_unit(STAGES - 1, PEER_HEADS - 1, NT - 1)


_INS = ['x', 'sb_norm', 'sb_w_qkv', 'sb_w_o', 'sw_norm', 'sw_w_qkv', 'sw_q_gain', 'sw_k_gain', 'sw_sinks', 'sw_w_o',
        'ffn_norm', 'peer_w_query', 'peer_sub_keys', 'peer_u', 'peer_v']
_OUT = ((1, S, D), 'float32')


def kernel(**inputs):
    import concourse.bacc as bacc
    from concourse.bass_utils import run_bass_kernel_spmd

    nc = bacc.Bacc("TRN2", target_bir_lowering=False, num_devices=1)
    arrays, args = {}, []
    for name in _INS:
        a = np.ascontiguousarray(inputs[name])
        arrays[f"in_{name}"] = a
        args.append(nc.dram_tensor(f"in_{name}", a.shape, mybir.dt.from_np(a.dtype), kind="ExternalInput").ap())
    shape, dtype = _OUT
    args.append(nc.dram_tensor("out_h", shape, mybir.dt.from_np(np.dtype(dtype)), kind="ExternalOutput").ap())
    build(nc, *args)
    r = run_bass_kernel_spmd(nc, [arrays], core_ids=[0])
    return r.results[0]["out_h"]
```

```python
from contextlib import ExitStack

import concourse.bass as bass
import numpy as np
from concourse import mybir

F32 = mybir.dt.float32
BF16 = mybir.dt.bfloat16
U32 = mybir.dt.uint32
ALU = mybir.AluOpType
ACT = mybir.ActivationFunctionType
AX_X = mybir.AxisListType.X

P = 128
D = 1024
S = 512
TT = S // P
NT = 2
NS = NT * P
KC = D // P
BANK = 512
HALVES = D // BANK
DH = 64
SCALE = DH ** -0.5
PAIRS = D // P
STEPS = 2 * NT
KV_PAIRS = 2
GROUP = 4
SW_HEADS = 16
WIN = 2 * P
PEER_HEADS = 8
KEYS = 128
TOPK = 16
TOP8 = 8
STAGES = 4
UNITS = PEER_HEADS * NT
LAST_ROWS = 11
SLOTS = 8
PROJ = 3
CREDIT = 1
RMS_EPS = 1e-6
MASKED = -1.0e30
LOWEST = -3.0e38
HUGE = 3.0e37
GELU_C = 2.0 * (2.0 / np.pi) ** 0.5
GELU_A = 0.044715


def spread(ap, axis, shape):
    return ap.unsqueeze(axis).broadcast_to(shape)


def first_tile(s):
    return NT * (s % 2)


def segments(s):
    return [(0, 1), (1, 4), (4, 5), (5, 7), (7, 8)] if s in (1, 2) else [(0, 1), (1, 7), (7, 8)]


def build(nc, x, sb_norm, sb_w_qkv, sb_w_o, sw_norm, sw_w_qkv, sw_q_gain, sw_k_gain, sw_sinks, sw_w_o,
          ffn_norm, peer_w_query, peer_sub_keys, peer_u, peer_v, out):
    x_tiles = x[0].rearrange("(t p) d -> t p d", p=P)
    out_tiles = out[0].rearrange("(t p) d -> t p d", p=P)
    kv_kept = nc.dram_tensor("kv_kept", (PAIRS, P, 2, NS), F32, kind="Internal").ap()

    with ExitStack() as ctx:
        def sb(name, shape, dt=F32):
            return ctx.enter_context(nc.sbuf_tensor(name, shape, dt))

        def sem(name):
            return ctx.enter_context(nc.semaphore(name))

        h = sb("h", [P, TT, D])
        xn = sb("xn", [P, TT, D])
        attn_xT = sb("attn_xT", [P, KC, NS])
        peer_xT = sb("peer_xT", [P, KC, NS])
        gain_b = sb("gain_b", [P, 2, D])
        sumsq = sb("sumsq", [P, NT])
        root = sb("root", [P, NT])
        rstd = sb("rstd", [P, NT])
        eps = sb("eps", [P, 1])
        sqrt_set = sb("sqrt_set", [P, 1])
        ident = sb("ident", [P, P])
        ident_bf = sb("ident_bf", [P, P], BF16)
        later_bf = sb("later_bf", [P, P], BF16)
        slot_no = sb("slot_no", [P, TOPK])
        dist = sb("dist", [P, WIN])
        neg_slope = sb("neg_slope", [P, SW_HEADS])
        w_queries = sb("w_queries", [P, KC, 2 * GROUP * DH])
        w_q = w_queries[:, :, 0:P]
        w_k = sb("w_k", [P, KC, P])
        w_v = sb("w_v", [P, KC, P])
        wo = sb("wo", [P, D])
        qT = sb("qT", [P, NS])
        WIN_COLS = KV_PAIRS * (NT + 1) * P
        kv_mem = sb("kv_mem", [P, 2 * WIN_COLS])
        kT = kv_mem[:, 0:S]
        v_tok = kv_mem[:, S:2 * S].rearrange("p (t c) -> p t c", c=P)
        kT_win = kv_mem[:, 0:WIN_COLS].rearrange("p (j s) -> p j s", j=KV_PAIRS)
        v_win = kv_mem[:, WIN_COLS:2 * WIN_COLS].rearrange("p (j t c) -> p j t c", j=KV_PAIRS, c=P)
        oT = sb("oT", [P, NS])
        work = sb("work", [P, 8 * BANK + 2])
        fail = work[:, 0:2 * BANK].rearrange("p (r s) -> p r s", r=2)
        take = work[:, 2 * BANK:4 * BANK].rearrange("p (r s) -> p r s", r=2)
        attn = work[:, 4 * BANK:6 * BANK].rearrange("p (r s) -> p r s", r=2)
        left = work[:, 6 * BANK:8 * BANK + 2].rearrange("p (r s) -> p r s", r=2)
        sw_score = work[:, 0:2 * BANK].rearrange("p (a n w) -> p a n w", a=2, n=NT)
        prob = work[:, 2 * BANK:4 * BANK].rearrange("p (a n w) -> p a n w", a=2, n=NT)
        head_tok = work[:, 4 * BANK:5 * BANK]
        head_sq = work[:, 5 * BANK:6 * BANK]
        attnT = sb("attnT", [P, 2, BANK])
        qk_gain = sb("qk_gain", [P, 2, DH])
        sink_b = sb("sink_b", [P, SW_HEADS])
        head_ss = sb("head_ss", [P, 4 * NT])
        head_root = sb("head_root", [P, 4 * NT])
        head_rstd = sb("head_rstd", [P, 4 * NT])
        top = sb("top", [P, 2, NT])
        neg_top = sb("neg_top", [P, 2, NT])
        sink_arg = sb("sink_arg", [P, 2, NT])
        sink_exp = sb("sink_exp", [P, 2, NT])
        row_sum = sb("row_sum", [P, 2, NT])
        denom = sb("denom", [P, 2, NT])
        inv_denom = sb("inv_denom", [P, 2, NT])
        u_ring = sb("u_ring", [P, SLOTS, D])
        v_ring = sb("v_ring", [P, SLOTS, D])
        w_pq = sb("w_pq", [P, KC, 2 * P])
        keys = sb("keys", [P, 2, P])
        keysT = sb("keysT", [P, 2, P])
        pqT = sb("pqT", [P, 2, NS])
        scores = sb("scores", [P, NT, 2, KEYS])
        rest = sb("rest", [P, 2, KEYS])
        half_top = sb("half_top", [P, 2, TOPK])
        half_idx = sb("half_idx", [P, 2, TOPK], U32)
        half_idx_f = sb("half_idx_f", [P, 2, TOPK])
        cand = sb("cand", [P, TOPK, TOPK])
        cand_rest = sb("cand_rest", [P, TOPK * TOPK])
        cand_top = sb("cand_top", [P, TOPK])
        cand_idx = sb("cand_idx", [P, TOPK], U32)
        place = sb("place", [P, 2, TOPK], U32)
        place_f = sb("place_f", [P, 2, TOPK])
        onehot = sb("onehot", [P, 2, TOPK, TOPK])
        picked = sb("picked", [P, 2, TOPK])
        expert = sb("expert", [P, NT, TOPK], U32)
        neg_best = sb("neg_best", [P, 1])
        gate = sb("gate", [P, TOPK])
        gate_sum = sb("gate_sum", [P, 1])
        inv_gate = sb("inv_gate", [P, 1])
        hid = sb("hid", [P, TOPK])
        g1 = sb("g1", [P, TOPK])
        g2 = sb("g2", [P, TOPK])
        g3 = sb("g3", [P, TOPK])
        gelu_exp = sb("gelu_exp", [P, TOPK])
        coef = sb("coef", [P, TOPK])
        diag = sb("diag", [P, TOPK, P])

        acc = [ctx.enter_context(nc.psum_tensor(f"acc{c}", [P, BANK], F32)) for c in range(HALVES)]
        x_cur = ctx.enter_context(nc.psum_tensor("x_cur", [P, D], F32))
        qk_bank = ctx.enter_context(nc.psum_tensor("qk_bank", [P, BANK], F32))
        vo_bank = ctx.enter_context(nc.psum_tensor("vo_bank", [P, BANK], F32))
        z_own = ctx.enter_context(nc.psum_tensor("z_bank", [P, BANK], F32))
        t_own = ctx.enter_context(nc.psum_tensor("t_bank", [P, BANK], F32))
        o_part = vo_bank[:, NS:2 * NS]
        qT_sets = [qT[:], u_ring[:, 0, 0:NS]]
        kT_sets = [kT, u_ring[:, 0, NS:2 * NS]]
        v_sets = [v_tok, u_ring[:, 0, 2 * NS:3 * NS].rearrange("p (t c) -> p t c", c=P)]
        o_banks = {0: x_cur[:, 0:NS], 1: o_part}
        z_banks = {0: [z_own[:], acc[0][:]], 1: [z_own[:]] * 2}
        t_banks = {0: [t_own[:], acc[1][:]], 1: [t_own[:]] * 2}

        x_landed = [sem("x_landed0"), sem("x_landed1")]
        attn_gain_landed = sem("attn_gain_landed")
        peer_gain_landed = sem("peer_gain_landed")
        small_landed = sem("small_landed")
        pool_step = sem("pool_step")
        const_ready = sem("const_ready")
        sumsq_ready = sem("sumsq_ready")
        root_ready = sem("root_ready")
        xn_ready = sem("xn_ready")
        xT_done = sem("xT_done")
        xT_ready = sem("xT_ready")
        wqkv_landed = [sem("w_q_landed"), sem("w_k_landed"), sem("w_v_landed")]
        kept_landed = sem("kept_landed")
        kv_stored = sem("kv_stored")
        wo_landed = [sem("wo_landed0"), sem("wo_landed1")]
        proj_done = sem("proj_done")
        proj_copied = sem("proj_copied")
        z_done = sem("z_done")
        gates_ready = sem("gates_ready")
        left_ready = sem("left_ready")
        attn_ready = sem("attn_ready")
        attnT_done = sem("attnT_done")
        attnT_ready = sem("attnT_ready")
        o_done = sem("o_done")
        oT_ready = sem("oT_ready")
        wo_done = sem("wo_done")
        h_added = sem("h_added")
        dve_set = sem("dve_set")
        wkv_landed = sem("wkv_landed")
        wq_landed = sem("wq_landed")
        q_done = sem("q_done")
        kv_done = sem("kv_done")
        q_copied = sem("q_copied")
        kept_copied = sem("kept_copied")
        headss_ready = sem("headss_ready")
        headroot_ready = sem("headroot_ready")
        headn_ready = sem("headn_ready")
        headT_done = sem("headT_done")
        headT_ready = sem("headT_ready")
        swz_done = sem("swz_done")
        swz_read = sem("swz_read")
        negtop_ready = sem("negtop_ready")
        exp_ready = sem("exp_ready")
        prob_ready = sem("prob_ready")
        probT_done = sem("probT_done")
        probT_ready = sem("probT_ready")
        swo_done = sem("swo_done")
        swoT_ready = sem("swoT_ready")
        wpq_landed = sem("wpq_landed")
        keysT_done = sem("keysT_done")
        keysT_ready = sem("keysT_ready")
        pq_done = sem("pq_done")
        pqT_ready = sem("pqT_ready")
        score_done = sem("score_done")
        scores_ready = sem("scores_ready")
        best_ready = sem("best_ready")
        gate_ready = sem("gate_ready")
        expert_ready = sem("expert_ready")
        gather_turn = sem("gather_turn")
        u_landed = [sem(f"u_landed{s}") for s in range(SLOTS)]
        v_landed = [sem(f"v_landed{s}") for s in range(SLOTS)]
        u_slots_free = sem("u_slots_free")
        v_slots_free = sem("v_slots_free")
        gelu_arg_ready = sem("gelu_arg_ready")
        gelu_exp_ready = sem("gelu_exp_ready")
        coef_ready = sem("coef_ready")
        diag_ready = sem("diag_ready")
        acc_added = sem("acc_added")
        dve_step = sem("dve_step")
        out_stored = sem("out_stored")

        block = ctx.enter_context(nc.Block())

        def run(eng, s, iteration):
            for lo, hi in segments(s):
                if hi - lo == 1:
                    iteration(lo, lo == 0, hi == PEER_HEADS, lo)
                else:
                    with eng.Fori(lo, hi) as hd:
                        iteration(hd, False, False, lo)

        @block.sync
        def _(sp):
            w3 = sb_w_qkv[0].rearrange("(k p) n -> p k n", p=P)
            w2 = sw_w_qkv[0].rearrange("(k p) n -> p k n", p=P)
            wo0 = sb_w_o[0].rearrange("(i p) n -> p i n", p=P)
            wo1 = sw_w_o[0].rearrange("(j a g p) n -> a p j g n", j=KV_PAIRS, a=2, g=GROUP)

            def load_peer(s, hd):
                wq3 = peer_w_query[s // 2].rearrange("(k p) n -> p k n", p=P)
                sk = peer_sub_keys[s // 2].rearrange("h s n c -> n h s c")
                sp.wait_ge(pq_done, hd * 2 + (s * 2 * PEER_HEADS + CREDIT))
                sp.dma_start(w_pq[:], wq3[:, :, bass.ds(hd * 2 * P, 2 * P)]).then_inc(wpq_landed, 16)
                sp.dma_start(keys[:], sk[:, bass.ds(hd, 1), :, :].squeeze(1)).then_inc(wpq_landed, 16)

            def load_pair0(p, i):
                for sec, w in enumerate((w_q, w_k, w_v)):
                    sp.wait_ge(proj_done, i * PROJ + (PROJ * PAIRS * p + sec + 1))
                    sp.dma_start(w[:], w3[:, :, bass.ds(i * P + sec * D, P)]).then_inc(wqkv_landed[sec], 16)
                if p:
                    sp.wait_ge(o_done, i * STEPS + STEPS * PAIRS)
                    kept = kv_kept[bass.ds(i, 1)].squeeze(0)
                    sp.dma_start(kT[:, 0:NS], kept[:, 0, :]).then_inc(kept_landed, 16)
                    sp.dma_start(v_tok[:, 0:NT, :].rearrange("p t c -> p (t c)"), kept[:, 1, :]).then_inc(kept_landed, 16)

            def load_wo0(p, i):
                sp.wait_ge(wo_done, i * NT + (NT * PAIRS * p + CREDIT))
                sp.dma_start(wo[:], wo0[:, bass.ds(i, 1), :].squeeze(1)).then_inc(wo_landed[0], 16)

            def load_pair1(p, i, lo):
                if lo in (0, GROUP):
                    j = lo // GROUP
                    sp.wait_ge(kv_done, 2 * (KV_PAIRS * (p % 2) + j) + CREDIT)
                    sp.dma_start(w_k[:], w2[:, :, D + j * P:D + (j + 1) * P]).then_inc(wkv_landed, 16)
                    sp.dma_start(w_v[:], w2[:, :, D + (KV_PAIRS + j) * P:D + (KV_PAIRS + j + 1) * P]).then_inc(wkv_landed, 16)
                    sp.wait_ge(q_done, i + (PAIRS * (p % 2) + CREDIT))
                    sp.dma_start(w_queries[:], w2[:, :, 2 * GROUP * DH * j:2 * GROUP * DH * (j + 1)]).then_inc(wq_landed, 16)

            def load_wo1(p, i, lo):
                j = lo // GROUP
                sp.wait_ge(wo_done, i * NT + (NT * PAIRS * p + CREDIT))
                for a in range(2):
                    sp.dma_start(wo[a * DH:(a + 1) * DH, :],
                                 wo1[a][:, j, bass.ds(i - GROUP * j, 1), :].squeeze(1)).then_inc(wo_landed[1], 16)

            def store_kv(i, b):
                sp.wait_ge(proj_copied, i * PROJ + PROJ)
                kept = kv_kept[bass.ds(i, 1)].squeeze(0)
                sp.dma_start(kept[:, 0, :], kT_sets[b][:, 0:NS]).then_inc(kv_stored, 16)
                sp.dma_start(kept[:, 1, :].rearrange("p (t c) -> p t c", c=P), v_sets[b][:, 0:NT, :]).then_inc(kv_stored, 16)

            for t in range(NT):
                sp.dma_start(h[:, t, :], x_tiles[t]).then_inc(x_landed[0], 16)
            sp.dma_start(gain_b[:, 0, :], sb_norm[0:1, :].broadcast_to([P, D])).then_inc(attn_gain_landed, 16)
            load_pair0(0, 0)
            for t in range(NT, TT):
                sp.dma_start(h[:, t, :], x_tiles[t]).then_inc(x_landed[1], 16)
            with sp.Fori(0, PAIRS // 2 - 1) as ii:
                for b in range(2):
                    load_pair0(0, ii * 2 + (b + 1))
                    load_wo0(0, ii * 2 + b)
                    store_kv(ii * 2 + b, b)
            load_pair0(0, PAIRS - 1)
            for b in range(2):
                load_wo0(0, PAIRS - 2 + b)
                store_kv(PAIRS - 2 + b, b)
            sp.wait_ge(kv_stored, 32 * PAIRS + CREDIT)
            sp.dma_start(gain_b[:, 1, :], ffn_norm[0:1, :].broadcast_to([P, D])).then_inc(peer_gain_landed, 16)
            sp.dma_start(qk_gain[:, 0, :], sw_q_gain[0:1, :].broadcast_to([P, DH])).then_inc(small_landed, 16)
            sp.dma_start(qk_gain[:, 1, :], sw_k_gain[0:1, :].broadcast_to([P, DH])).then_inc(small_landed, 16)
            sp.dma_start(sink_b[:], sw_sinks[0:1, :].broadcast_to([P, SW_HEADS])).then_inc(small_landed, 16)
            load_peer(0, 0)
            for s in range(STAGES):
                p = s + 1
                if p == 2:
                    sp.wait_ge(proj_done, PROJ * PAIRS * 2 + PROJ)

                def iteration(hd, first, last, lo):
                    if p == 1:
                        load_pair0(p, hd)
                    elif p < STAGES:
                        load_pair1(p, hd, lo)
                    if not last:
                        load_peer(s, hd + 1)
                    elif p < STAGES:
                        load_peer(s + 1, 0)
                    if p == 1:
                        load_wo0(p, hd)
                    elif p < STAGES:
                        load_wo1(p, hd, lo)
                    if first and s == 0:
                        sp.wait_ge(xn_ready, 3 * NT)
                        sp.dma_start(gain_b[:, 0, :], sw_norm[0:1, :].broadcast_to([P, D])).then_inc(attn_gain_landed, 16)
                    if first and s == 1:
                        sp.wait_ge(xn_ready, 4 * NT)
                        sp.dma_start(gain_b[:, 1, :], ffn_norm[1:2, :].broadcast_to([P, D])).then_inc(peer_gain_landed, 16)

                run(sp, s, iteration)
                if s >= 2:
                    for t in range(NT):
                        sp.wait_ge(acc_added, UNITS * (s + 1) - NT + t + 1)
                        sp.dma_start(out_tiles[first_tile(s) + t], h[:, first_tile(s) + t, :]).then_inc(out_stored, 16)
            sp.wait_ge(out_stored, 16 * TT)

        @block.gpsimd
        def _(pool):
            pool.memset(eps[:], RMS_EPS).then_inc(const_ready, 1)
            pool.memset(ident[:], 0.0).then_inc(pool_step, 1)
            pool.memset(ident_bf[:], 0.0).then_inc(pool_step, 1)
            pool.memset(later_bf[:], MASKED).then_inc(pool_step, 1)
            pool.iota(dist[:], pattern=[[-1, WIN]], base=P, channel_multiplier=1,
                      allow_small_or_imprecise_dtypes=True).then_inc(pool_step, 1)
            pool.wait_ge(pool_step, 4)
            for m in (ident, ident_bf):
                pool.affine_select(out=m[:], in_=m[:], compare_op=ALU.not_equal, fill=1.0, base=0,
                                   pattern=[[-1, P]], channel_multiplier=1).then_inc(const_ready, 1)
            pool.affine_select(out=later_bf[:], in_=later_bf[:], compare_op=ALU.is_ge, fill=0.0, base=0,
                               pattern=[[1, P]], channel_multiplier=-1).then_inc(const_ready, 1)
            pool.affine_select(out=dist[:], in_=dist[:], compare_op=ALU.is_ge, fill=-MASKED, base=P,
                               pattern=[[-1, WIN]], channel_multiplier=1).then_inc(pool_step, 1)
            pool.wait_ge(pool_step, 5)
            pool.affine_select(out=dist[:], in_=dist[:], compare_op=ALU.is_gt, fill=-MASKED, base=0,
                               pattern=[[1, WIN]], channel_multiplier=-1).then_inc(const_ready, 1)
            pool.iota(slot_no[:], pattern=[[1, TOPK]], base=0, channel_multiplier=0,
                      allow_small_or_imprecise_dtypes=True).then_inc(const_ready, 1)
            for hd in range(SW_HEADS):
                pool.memset(neg_slope[:, hd:hd + 1], -2.0 ** (-8.0 * (hd + 1) / SW_HEADS)).then_inc(const_ready, 1)

            for s in range(STAGES):
                with pool.Fori(0, PEER_HEADS) as hd:
                    for t in range(NT):
                        first = UNITS * s + t
                        pool.wait_ge(expert_ready, hd * NT + (first + 1))
                        pool.sem_inc(gather_turn, 1)
                        for table, ring, landed, free in ((peer_u, u_ring, u_landed, u_slots_free),
                                                          (peer_v, v_ring, v_landed, v_slots_free)):
                            for k in range(TOPK):
                                pool.wait_ge(free, hd * (NT * TOPK) + (first * TOPK + k + 1))
                                pool.sem_inc(gather_turn, 1)
                                pool.indirect_dma_start(
                                    ring[:, k % SLOTS, :], None, table.rearrange("l e d -> (l e) d"),
                                    bass.IndirectOffsetOnAxis(ap=expert[:, t, k:k + 1], axis=0),
                                    element_offset=(s // 2) * KEYS * KEYS * D).then_inc(landed[k % SLOTS], 16)

        CONSTS = 6 + SW_HEADS

        @block.scalar
        def _(act):
            def norm_roots(m, s):
                act.activation(sqrt_set[:], eps[:], ACT.Sqrt)
                for n in range(NT):
                    if m % 2:
                        act.wait_ge(h_added, NT * PAIRS * (s + 1) - NT + n + 1 + CREDIT)
                    act.activation(xn[:, first_tile(s) + n, :], h[:, first_tile(s) + n, :], ACT.Square,
                                   accum_out=sumsq[:, n:n + 1]).then_inc(sumsq_ready, 1)
                act.wait_ge(sumsq_ready, NT * (m + 1))
                act.activation(root[:], sumsq[:], ACT.Sqrt, bias=eps[:], scale=1.0 / D).then_inc(root_ready, 1)

            def norm_copies(m, xT):
                for n in range(NT):
                    for b, bank in enumerate((z_own, t_own)):
                        act.wait_ge(xT_done, 2 * (NT * m + n) + b + 1)
                        act.activation(xT[:, 4 * b:4 * b + 4, n * P:(n + 1) * P],
                                       bank[:].rearrange("p (k s) -> p k s", k=4), ACT.Copy).then_inc(xT_ready, 1)

            def copy_qk0(p, i, b=0):
                lo = first_tile(p)
                act.wait_ge(proj_done, i * PROJ + (PROJ * (PAIRS * p + 1) + 2))
                if p == 0:
                    act.wait_ge(kv_stored, i * 32 + CREDIT)
                act.activation(qT_sets[b], qk_bank[:, 0:NS], ACT.Copy).then_inc(proj_copied, 1)
                act.activation(kT_sets[b][:, lo * P:lo * P + NS], qk_bank[:, NS:2 * NS], ACT.Copy).then_inc(proj_copied, 1)

            def copy_v0(p, i, b=0):
                lo = first_tile(p)
                act.wait_ge(proj_done, i * PROJ + (PROJ * (PAIRS * p + 1) + 3))
                act.activation(v_sets[b][:, lo:lo + NT, :], vo_bank[:, 0:NS].rearrange("p (t c) -> p t c", c=P),
                               ACT.Copy).then_inc(proj_copied, 1)

            def gates0(p, i, u):
                w = (first_tile(p) + u % NT + 1) * P
                z = z_banks[p][u % 2]
                act.wait_ge(z_done, i * STEPS + (STEPS * PAIRS * p + u + 1))
                if u >= 2:
                    act.wait_ge(attn_ready, i * STEPS + (STEPS * PAIRS * p + u - 1))
                act.activation(fail[:, u % 2, 0:w], z[:, 0:w], ACT.Sigmoid, scale=-SCALE)
                act.activation(take[:, u % 2, 0:w], z[:, 0:w], ACT.Sigmoid, scale=SCALE).then_inc(gates_ready, 1)

            def copy_attnT0(p, i, u):
                w = (first_tile(p) + u % NT + 1) * P
                act.wait_ge(attnT_done, i * STEPS + (STEPS * PAIRS * p + u + 1))
                act.activation(attnT[:, u % 2, 0:w], t_banks[p][u % 2][:, 0:w], ACT.Copy).then_inc(attnT_ready, 1)

            def copy_o0(p, i, a):
                rows = slice(a * DH, (a + 1) * DH)
                act.wait_ge(o_done, i * STEPS + (STEPS * PAIRS * p + NT * (a + 1)))
                act.activation(oT[rows, :], o_banks[p][rows, :], ACT.Copy).then_inc(oT_ready, 1)

            def copy_proj1(p, i, lo):
                j = lo // GROUP
                if lo in (0, GROUP):
                    if p % 2:
                        act.activation(kT_win[:, j, 0:P], kT_win[:, j, NT * P:(NT + 1) * P], ACT.Copy).then_inc(kept_copied, 1)
                        act.activation(v_win[:, j, 0, :], v_win[:, j, NT, :], ACT.Copy).then_inc(kept_copied, 1)
                        act.wait_ge(kept_copied, 2 * (j + 1))
                    act.wait_ge(kv_done, 2 * (KV_PAIRS * (p % 2) + j + 1) + CREDIT)
                    act.activation(v_win[:, j, 1:NT + 1, :].rearrange("p t c -> p (t c)"), vo_bank[:, 0:NS],
                                   ACT.Copy)
                w = 2 * NS if lo in (0, GROUP) else NS
                act.wait_ge(q_done, i + (PAIRS * (p % 2) + 1 + CREDIT))
                act.activation(head_tok[:, 0:w], qk_bank[:, 0:w], ACT.Copy)
                act.activation(head_sq[:, 0:w], qk_bank[:, 0:w], ACT.Square).then_inc(q_copied, 1)

            def root1(p, i, lo):
                n = 4 * NT if lo in (0, GROUP) else 2 * NT
                act.wait_ge(headss_ready, i + (PAIRS * (p % 2) + 1))
                act.activation(head_root[:, 0:n], head_ss[:, 0:n], ACT.Sqrt, bias=eps[:],
                               scale=1.0 / DH).then_inc(headroot_ready, 1)

            def copy_headT1(p, i, lo):
                j = lo // GROUP
                act.wait_ge(headT_done, i + (PAIRS * (p % 2) + 1))
                if lo in (0, GROUP):
                    act.activation(kT_win[:, j, P:(NT + 1) * P], t_own[:, NS:2 * NS], ACT.Copy)
                act.activation(qT[:], t_own[:, 0:NS], ACT.Copy).then_inc(headT_ready, 1)

            def exp1(p, i, a):
                act.wait_ge(negtop_ready, i * 2 + (2 * PAIRS * (p % 2) + a + 1))
                for n in range(NT):
                    c = P if p % 2 == 0 and n == 0 else 0
                    act.activation(prob[:, a, n, c:WIN], sw_score[:, a, n, c:WIN], ACT.Exp,
                                   bias=neg_top[:, a, n:n + 1], accum_out=row_sum[:, a, n:n + 1])
                act.activation(sink_exp[:, a, :], sink_arg[:, a, :], ACT.Exp).then_inc(exp_ready, 1)

            def copy_probT1(p, i, a):
                act.wait_ge(probT_done, i * 2 + (2 * PAIRS * (p % 2) + a + 1))
                w0 = P if p % 2 == 0 else 0
                act.activation(attnT[:, a, w0:2 * WIN], t_own[:, w0:2 * WIN], ACT.Copy).then_inc(probT_ready, 1)

            def copy_o1(p, i, a):
                rows = slice(a * DH, (a + 1) * DH)
                act.wait_ge(swo_done, i * 2 + (2 * PAIRS * (p % 2) + a + 1))
                act.activation(oT[rows, :], o_part[rows, :], ACT.Copy).then_inc(swoT_ready, 1)

            def copy_outputs1(p, i):
                for a in range(2):
                    copy_probT1(p, i, a)
                    copy_o1(p, i, a)

            def copy_scores(s, hd):
                copy_keysT(s, hd)
                copy_queries_scores(s, hd)

            def copy_keysT(s, hd):
                act.wait_ge(keysT_done, hd + (s * PEER_HEADS + 1))
                act.activation(keysT[:].rearrange("p a b -> p (a b)"), vo_bank[:, 0:2 * P],
                               ACT.Copy).then_inc(keysT_ready, 1)

            def copy_queries_scores(s, hd):
                act.wait_ge(pq_done, hd * 2 + (s * 2 * PEER_HEADS + 2 + CREDIT))
                act.activation(pqT[:].rearrange("p a s -> p (a s)"), qk_bank[:], ACT.Copy).then_inc(pqT_ready, 1)
                act.wait_ge(score_done, hd + (s * PEER_HEADS + 1))
                act.activation(scores[:].rearrange("p t a n -> p (t a n)"), vo_bank[:], ACT.Copy).then_inc(scores_ready, 1)

            def unit_gate(s, hd, t):
                act.wait_ge(best_ready, hd * NT + (UNITS * s + t + 1))
                act.activation(gate[:], cand_top[:], ACT.Exp, bias=neg_best[:],
                               accum_out=gate_sum[:]).then_inc(gate_ready, 1)

            def unit_diag(s, hd, t):
                n = hd * NT + (UNITS * s + t + 1)
                act.wait_ge(gelu_arg_ready, n)
                act.activation(gelu_exp[:], g3[:], ACT.Exp).then_inc(gelu_exp_ready, 1)
                act.wait_ge(coef_ready, n)
                act.wait_ge(v_slots_free, hd * (NT * TOPK) + ((UNITS * s + t) * TOPK + SLOTS))
                for k in range(TOPK):
                    act.activation(diag[:, k, :], ident[:], ACT.Copy, scale=coef[:, k:k + 1]).then_inc(diag_ready, 1)

            act.sem_inc(kv_stored, CREDIT)
            act.wait_ge(const_ready, CONSTS)
            act.wait_ge(x_landed[0], 16 * NT)
            norm_roots(0, 0)
            norm_copies(0, attn_xT)

            def first_pair(i, b, more):
                gates0(0, i, 0)
                gates0(0, i, 1)
                copy_attnT0(0, i, 0)
                copy_attnT0(0, i, 1)
                gates0(0, i, 2)
                gates0(0, i, 3)
                if more:
                    copy_qk0(0, i + 1, 1 - b)
                copy_o0(0, i, 0)
                copy_attnT0(0, i, 2)
                copy_attnT0(0, i, 3)
                copy_o0(0, i, 1)
                if more:
                    copy_v0(0, i + 1, 1 - b)

            copy_qk0(0, 0)
            copy_v0(0, 0)
            with act.Fori(0, PAIRS // 2 - 1) as ii:
                first_pair(ii * 2, 0, True)
                first_pair(ii * 2 + 1, 1, True)
            first_pair(PAIRS - 2, 0, True)
            first_pair(PAIRS - 1, 1, False)
            act.wait_ge(x_landed[1], 16 * (TT - NT))
            for s in range(STAGES):
                p = s + 1
                if s == 0:
                    norm_roots(1, 0)
                    copy_keysT(0, 0)
                    norm_copies(1, peer_xT)
                    copy_queries_scores(0, 0)
                if p < STAGES:
                    if s:
                        act.wait_ge(acc_added, UNITS * s)
                    norm_roots(2 * s + 2, p)
                    norm_copies(2 * s + 2, attn_xT)

                def iteration(hd, first, last, lo):
                    turn = last and p < STAGES
                    unit_gate(s, hd, 0)
                    if p == 1:
                        copy_qk0(p, hd)
                        copy_v0(p, hd)
                    elif p < STAGES and not first:
                        copy_proj1(p, hd, lo)
                    if turn and p > 1:
                        root1(p, hd, lo)
                    if p == 1:
                        gates0(p, hd, 0)
                        gates0(p, hd, 1)
                    unit_diag(s, hd, 0)
                    if p == 1:
                        copy_attnT0(p, hd, 0)
                        if turn:
                            gates0(p, hd, 2)
                        copy_attnT0(p, hd, 1)
                        if turn:
                            gates0(p, hd, 3)
                        copy_o0(p, hd, 0)
                        if turn:
                            copy_attnT0(p, hd, 2)
                            copy_attnT0(p, hd, 3)
                            copy_o0(p, hd, 1)
                    elif p < STAGES:
                        if first:
                            copy_proj1(p, hd, lo)
                        if not turn:
                            root1(p, hd, lo)
                        copy_headT1(p, hd, lo)
                        if turn:
                            exp1(p, hd, 0)
                            exp1(p, hd, 1)
                            copy_outputs1(p, hd)
                    unit_gate(s, hd, 1)
                    if turn:
                        norm_roots(2 * p + 1, p)
                        copy_keysT(p, 0)
                        norm_copies(2 * p + 1, peer_xT)
                    if not last:
                        copy_scores(s, hd + 1)
                    if p == 1 and not turn:
                        gates0(p, hd, 2)
                        gates0(p, hd, 3)
                    elif p < STAGES and not turn:
                        exp1(p, hd, 0)
                    unit_diag(s, hd, 1)
                    if turn:
                        copy_queries_scores(p, 0)
                    elif p == 1:
                        copy_attnT0(p, hd, 2)
                        copy_attnT0(p, hd, 3)
                        copy_o0(p, hd, 1)
                    elif p < STAGES:
                        exp1(p, hd, 1)
                        copy_outputs1(p, hd)

                run(act, s, iteration)

        @block.tensor
        def _(pe):
            def norm(m, s, tiles=range(NT)):
                for n in tiles:
                    pe.wait_ge(xn_ready, NT * m + n + 1)
                    for b, bank in enumerate((z_own, t_own)):
                        if n >= 1:
                            pe.wait_ge(xT_ready, 2 * (NT * m + n - 1) + b + 1)
                        for k in range(4):
                            ins = pe.transpose(bank[:, k * P:(k + 1) * P],
                                               xn[:, first_tile(s) + n, (4 * b + k) * P:(4 * b + k + 1) * P], ident[:])
                        ins.then_inc(xT_done, 1)

            def project_T(dst, w, xT):
                for k in range(KC):
                    ins = pe.matmul(dst, w[:, k, :], xT[:, k, :], start=(k == 0), stop=(k == KC - 1))
                return ins

            def project(dst, w, xT, tiles=range(NT)):
                for n in tiles:
                    for k in range(KC):
                        ins = pe.matmul(dst[:, n * P:(n + 1) * P], xT[:, k, n * P:(n + 1) * P], w[:, k, :],
                                        start=(k == 0), stop=(k == KC - 1))
                return ins

            def output(p, i, n, banks):
                layer = p // 2
                if n == 0:
                    ready, before = (oT_ready, 2 * PAIRS * p) if layer == 0 else (swoT_ready, 2 * PAIRS * (p % 2))
                    pe.wait_ge(wo_landed[layer], i * (16 + 16 * layer) + (16 + 16 * layer) * (PAIRS * (p % 2) + 1))
                    pe.wait_ge(ready, i * 2 + (before + 2))
                for c in range(HALVES):
                    ins = pe.matmul(banks[c], oT[:, n * P:(n + 1) * P], wo[:, c * BANK:(c + 1) * BANK],
                                    start=True, stop=True)
                ins.then_inc(wo_done, 1)

            def project_q0(p, i):
                pe.wait_ge(wqkv_landed[0], i * 16 + 16 * (PAIRS * p + 1))
                project_T(qk_bank[:, 0:NS], w_q, attn_xT).then_inc(proj_done, 1)

            def project_k0(p, i):
                pe.wait_ge(wqkv_landed[1], i * 16 + 16 * (PAIRS * p + 1))
                project_T(qk_bank[:, NS:2 * NS], w_k, attn_xT).then_inc(proj_done, 1)

            def project_v0(p, i, tiles=range(NT)):
                if tiles[0] == 0:
                    pe.wait_ge(wqkv_landed[2], i * 16 + 16 * (PAIRS * p + 1))
                ins = project(vo_bank, w_v, attn_xT, tiles)
                if tiles[-1] == NT - 1:
                    ins.then_inc(proj_done, 1)

            def z0(p, i, u, b=0):
                a, n = u // NT, u % NT
                rows = slice(a * DH, (a + 1) * DH)
                t = first_tile(p) + n
                z = z_banks[p][u % 2]
                if u == 0:
                    pe.wait_ge(proj_copied, i * PROJ + PROJ * (PAIRS * p + 1))
                    if p:
                        pe.wait_ge(kept_landed, i * 32 + 32)
                lag = 2 if p == 0 else 1
                if u >= lag:
                    pe.wait_ge(gates_ready, i * STEPS + (STEPS * PAIRS * p + u + 1 - lag))
                pe.matmul(z[:, 0:(t + 1) * P], qT_sets[b][rows, n * P:(n + 1) * P], kT_sets[b][rows, 0:(t + 1) * P],
                          start=True, stop=False, skip_group_check=True)
                pe.matmul(z[:, t * P:(t + 1) * P], ident_bf[:], later_bf[:],
                          start=False, stop=True, skip_group_check=True).then_inc(z_done, 1)

            def transpose0(p, i, u):
                t = first_tile(p) + u % NT
                pe.wait_ge(attn_ready, i * STEPS + (STEPS * PAIRS * p + u + 1))
                for kb in range(t + 1):
                    ins = pe.transpose(t_banks[p][u % 2][:, kb * P:(kb + 1) * P],
                                       attn[:, u % 2, kb * P:(kb + 1) * P], ident[:])
                ins.then_inc(attnT_done, 1)

            def apply0(p, i, u, b=0):
                a, n = u // NT, u % NT
                rows = slice(a * DH, (a + 1) * DH)
                t = first_tile(p) + n
                pe.wait_ge(attnT_ready, i * STEPS + (STEPS * PAIRS * p + u + 1))
                for kb in range(t + 1):
                    ins = pe.matmul(o_banks[p][rows, n * P:(n + 1) * P], v_sets[b][:, kb, rows],
                                    attnT[:, u % 2, kb * P:(kb + 1) * P], start=(kb == 0), stop=(kb == t))
                ins.then_inc(o_done, 1)

            def project1(p, i, lo):
                j = lo // GROUP
                if lo in (0, GROUP):
                    pe.wait_ge(wkv_landed, 32 * (KV_PAIRS * (p % 2) + j + 1))
                    project(qk_bank[:, NS:2 * NS], w_k, attn_xT).then_inc(kv_done, 1)
                    project(vo_bank, w_v, attn_xT).then_inc(kv_done, 1)
                pe.wait_ge(wq_landed, 16 * (KV_PAIRS * (p % 2) + j + 1))
                heads = w_queries[:].rearrange("p k (a g c) -> p k a g c", a=2, g=GROUP)
                for n in range(NT):
                    for k in range(KC):
                        ins = pe.matmul(qk_bank[:, n * P:(n + 1) * P].rearrange("p (a c) -> p a c", a=2),
                                        attn_xT[:, k, n * P:(n + 1) * P],
                                        heads[:, k, :, bass.ds(i - GROUP * j, 1), :].squeeze(2),
                                        start=(k == 0), stop=(k == KC - 1))
                ins.then_inc(q_done, 1)

            def transpose_heads1(p, i, lo):
                pe.wait_ge(headn_ready, i + (PAIRS * (p % 2) + 1))
                for n in range(2 * NT if lo in (0, GROUP) else NT):
                    ins = pe.transpose(t_own[:, n * P:(n + 1) * P], head_tok[:, n * P:(n + 1) * P], ident[:])
                ins.then_inc(headT_done, 1)

            def z1(p, i, a, lo):
                j = lo // GROUP
                rows = slice(a * DH, (a + 1) * DH)
                if a == 0:
                    pe.wait_ge(headT_ready, i + (PAIRS * (p % 2) + 1))
                else:
                    pe.wait_ge(swz_read, i * 2 + (2 * PAIRS * (p % 2) + 1))
                for n in range(NT):
                    c = P if p % 2 == 0 and n == 0 else 0
                    ins = pe.matmul(z_own[:, n * WIN + c:(n + 1) * WIN], qT[rows, n * P:(n + 1) * P],
                                    kT_win[rows, j, n * P + c:n * P + WIN], start=True, stop=True)
                ins.then_inc(swz_done, 1)

            def transpose1(p, i, a):
                pe.wait_ge(prob_ready, i * 2 + (2 * PAIRS * (p % 2) + a + 1))
                if a:
                    pe.wait_ge(probT_ready, i * 2 + (2 * PAIRS * (p % 2) + a))
                for n in range(NT):
                    for b in range(2):
                        if p % 2 == 0 and n == 0 and b == 0:
                            continue
                        ins = pe.transpose(t_own[:, n * WIN + b * P:n * WIN + (b + 1) * P],
                                           prob[:, a, n, b * P:(b + 1) * P], ident[:])
                ins.then_inc(probT_done, 1)

            def apply1(p, i, a, lo):
                j = lo // GROUP
                rows = slice(a * DH, (a + 1) * DH)
                pe.wait_ge(probT_ready, i * 2 + (2 * PAIRS * (p % 2) + a + 1))
                for n in range(NT):
                    blocks = [1] if p % 2 == 0 and n == 0 else [0, 1]
                    for b in blocks:
                        ins = pe.matmul(o_part[rows, n * P:(n + 1) * P], v_win[:, j, n + b, rows],
                                        attnT[:, a, n * WIN + b * P:n * WIN + (b + 1) * P],
                                        start=(b == blocks[0]), stop=(b == 1))
                ins.then_inc(swo_done, 1)

            def keys_T(s, hd):
                pe.wait_ge(wpq_landed, hd * 32 + 32 * (s * PEER_HEADS + 1))
                for half in range(2):
                    ins = pe.transpose(vo_bank[:, half * P:(half + 1) * P], keys[:, half, :], ident[:])
                ins.then_inc(keysT_done, 1)

            def score_head(s, hd):
                keys_T(s, hd)
                for half in range(2):
                    peer_query(half)
                peer_scores(s, hd)

            def peer_query(half):
                project_T(qk_bank[:, half * NS:(half + 1) * NS], w_pq[:, :, half * P:(half + 1) * P],
                          peer_xT).then_inc(pq_done, 1)

            def peer_scores(s, hd):
                pe.wait_ge(keysT_ready, hd + (s * PEER_HEADS + 1))
                pe.wait_ge(pqT_ready, hd + (s * PEER_HEADS + 1))
                for t in range(NT):
                    for half in range(2):
                        ins = pe.matmul(vo_bank[:, (2 * t + half) * P:(2 * t + half + 1) * P],
                                        pqT[:, half, t * P:(t + 1) * P], keysT[:, half, :], start=True, stop=True)
                ins.then_inc(score_done, 1)

            def unit(s, hd, t, k0, k1, rows=TOPK):
                n = UNITS * s + t
                if k0 == 0 and not (isinstance(hd, int) and n + hd * NT == 0):
                    pe.wait_ge(acc_added, hd * NT + n)
                for k in range(k0, k1):
                    pe.wait_ge(v_landed[k % SLOTS], hd * (NT * 32) + (n * 32 + 16 * (k // SLOTS + 1)))
                    pe.wait_ge(diag_ready, hd * (NT * TOPK) + (n * TOPK + k + 1))
                    for c in range(HALVES):
                        ins = pe.matmul(acc[c][:], diag[:, k, :], v_ring[:, k % SLOTS, c * BANK:(c + 1) * BANK],
                                        start=(k == 0), stop=(k == rows - 1), skip_group_check=True)
                    ins.then_inc(v_slots_free, 1)

            pe.sem_inc(v_slots_free, SLOTS)
            pe.sem_inc(proj_done, PROJ)
            for c in (q_done, kv_done, pq_done, wo_done):
                pe.sem_inc(c, CREDIT)
            pe.wait_ge(const_ready, CONSTS)
            norm(0, 0)
            pe.wait_ge(xT_ready, 2 * NT)

            def first_pair(i, b, more):
                z0(0, i, 0, b)
                z0(0, i, 1, b)
                if more:
                    project_q0(0, i + 1)
                pe.wait_ge(h_added, i * NT + CREDIT)
                transpose0(0, i, 0)
                transpose0(0, i, 1)
                z0(0, i, 2, b)
                z0(0, i, 3, b)
                if more:
                    project_k0(0, i + 1)
                apply0(0, i, 0, b)
                apply0(0, i, 1, b)
                transpose0(0, i, 2)
                transpose0(0, i, 3)
                if more:
                    project_v0(0, i + 1, [0])
                apply0(0, i, 2, b)
                apply0(0, i, 3, b)
                if more:
                    project_v0(0, i + 1, [1])
                output(0, i, 0, [t_own[:], acc[1][:]])
                if more:
                    pe.wait_ge(proj_copied, i * PROJ + 2 * PROJ)
                output(0, i, 1, [x_cur[:, BANK:D], vo_bank[:]])

            project_q0(0, 0)
            project_k0(0, 0)
            project_v0(0, 0)
            with pe.Fori(0, PAIRS // 2 - 1) as ii:
                first_pair(ii * 2, 0, True)
                first_pair(ii * 2 + 1, 1, True)
            first_pair(PAIRS - 2, 0, True)
            first_pair(PAIRS - 1, 1, False)
            pe.wait_ge(h_added, NT * PAIRS + CREDIT)
            for s in range(STAGES):
                p = s + 1
                if s == 0:
                    keys_T(0, 0)
                    norm(1, 0)
                    pe.wait_ge(xT_ready, 2 * NT * 2)
                    peer_query(0)
                    peer_query(1)
                    peer_scores(0, 0)
                if p < STAGES:
                    norm(2 * s + 2, p)
                    pe.wait_ge(xT_ready, 2 * NT * (2 * s + 3))
                pe.wait_ge(scores_ready, s * PEER_HEADS + 1)

                def iteration(hd, first, last, lo):
                    if p < STAGES and not first:
                        output(p, hd - 1, 0, [z_own[:], t_own[:]])
                    if p == 1:
                        project_q0(p, hd)
                        project_k0(p, hd)
                        project_v0(p, hd)
                        pe.wait_ge(proj_copied, hd * PROJ + PROJ * (PAIRS * p + 1))
                    elif p < STAGES and not first:
                        project1(p, hd, lo)
                        pe.wait_ge(q_copied, hd + (PAIRS * (p % 2) + 1))
                    if p < STAGES and not first:
                        output(p, hd - 1, 1, [qk_bank[:], vo_bank[:]])
                    if p == 1:
                        if not first:
                            pe.wait_ge(h_added, hd * NT + (NT * PAIRS * p - 1 + CREDIT))
                        z0(p, hd, 0)
                        z0(p, hd, 1)
                    turn = last and p < STAGES
                    banks_read = hd * NT + (NT * PAIRS * p + CREDIT)
                    if turn and p == 1:
                        unit(s, hd, 0, 0, 9)
                        pe.wait_ge(h_added, banks_read)
                        transpose0(p, hd, 0)
                        z0(p, hd, 2)
                        unit(s, hd, 0, 9, 11)
                        apply0(p, hd, 0)
                        transpose0(p, hd, 1)
                        z0(p, hd, 3)
                        unit(s, hd, 0, 11, 13)
                        apply0(p, hd, 1)
                        transpose0(p, hd, 2)
                        unit(s, hd, 0, 13, 15)
                        apply0(p, hd, 2)
                        transpose0(p, hd, 3)
                        unit(s, hd, 0, 15, TOPK)
                        apply0(p, hd, 3)
                    elif turn:
                        unit(s, hd, 0, 0, 3)
                        pe.wait_ge(h_added, banks_read)
                        transpose_heads1(p, hd, lo)
                        unit(s, hd, 0, 3, 6)
                        z1(p, hd, 0, lo)
                        unit(s, hd, 0, 6, 9)
                        z1(p, hd, 1, lo)
                        unit(s, hd, 0, 9, 12)
                        transpose1(p, hd, 0)
                        unit(s, hd, 0, 12, 14)
                        apply1(p, hd, 0, lo)
                        transpose1(p, hd, 1)
                        unit(s, hd, 0, 14, TOPK)
                        apply1(p, hd, 1, lo)
                    elif p == 1:
                        unit(s, hd, 0, 0, 9)
                        if not first:
                            pe.wait_ge(h_added, banks_read)
                        transpose0(p, hd, 0)
                        unit(s, hd, 0, 9, 11)
                        apply0(p, hd, 0)
                        unit(s, hd, 0, 11, 12)
                        transpose0(p, hd, 1)
                        unit(s, hd, 0, 12, 14)
                        apply0(p, hd, 1)
                        unit(s, hd, 0, 14, TOPK)
                    elif p < STAGES and first:
                        unit(s, hd, 0, 0, 9)
                        project1(p, hd, lo)
                        unit(s, hd, 0, 9, 15)
                        transpose_heads1(p, hd, lo)
                        unit(s, hd, 0, 15, TOPK)
                        z1(p, hd, 0, lo)
                    elif p < STAGES:
                        unit(s, hd, 0, 0, 10)
                        pe.wait_ge(h_added, banks_read)
                        transpose_heads1(p, hd, lo)
                        unit(s, hd, 0, 10, 14)
                        z1(p, hd, 0, lo)
                        unit(s, hd, 0, 14, TOPK)
                    else:
                        unit(s, hd, 0, 0, TOPK)
                    if not last:
                        if p == 1:
                            pe.wait_ge(oT_ready, hd * 2 + (2 * PAIRS * p + 1))
                        score_head(s, hd + 1)
                        pe.wait_ge(scores_ready, hd + (s * PEER_HEADS + 2))
                    if turn:
                        output(p, hd, 0, [z_own[:], t_own[:]])
                        output(p, hd, 1, [qk_bank[:], vo_bank[:]])
                    if turn:
                        pe.wait_ge(h_added, NT * PAIRS * (p + 1) + CREDIT)
                        keys_T(p, 0)
                        norm(2 * p + 1, p)
                        pe.wait_ge(xT_ready, 2 * NT * (2 * p + 2))
                        peer_query(0)
                        peer_query(1)
                        unit(s, hd, 1, 0, 2)
                        peer_scores(p, 0)
                        unit(s, hd, 1, 2, TOPK)
                    elif p == 1:
                        z0(p, hd, 2)
                        z0(p, hd, 3)
                        unit(s, hd, 1, 0, 9)
                        transpose0(p, hd, 2)
                        unit(s, hd, 1, 9, 11)
                        apply0(p, hd, 2)
                        unit(s, hd, 1, 11, 12)
                        transpose0(p, hd, 3)
                        unit(s, hd, 1, 12, 14)
                        apply0(p, hd, 3)
                        unit(s, hd, 1, 14, TOPK)
                    elif p < STAGES:
                        z1(p, hd, 1, lo)
                        unit(s, hd, 1, 0, 10)
                        transpose1(p, hd, 0)
                        unit(s, hd, 1, 10, 12)
                        apply1(p, hd, 0, lo)
                        unit(s, hd, 1, 12, 13)
                        transpose1(p, hd, 1)
                        unit(s, hd, 1, 13, TOPK)
                        apply1(p, hd, 1, lo)
                    elif last:
                        unit(s, hd, 1, 0, LAST_ROWS, LAST_ROWS)
                    else:
                        unit(s, hd, 1, 0, TOPK)

                run(pe, s, iteration)

        @block.vector
        def _(dve):
            def norm(m, s, which, landed, n_landed):
                dve.wait_ge(root_ready, m + 1)
                dve.sem_clear(dve_step)
                dve.reciprocal(rstd[:], root[:]).then_inc(dve_step, 1)
                dve.wait_ge(dve_step, 1)
                dve.wait_ge(landed, n_landed)
                for n in range(NT):
                    t = first_tile(s) + n
                    dve.scalar_tensor_tensor(out=xn[:, t, :], in0=h[:, t, :], scalar=rstd[:, n:n + 1],
                                             in1=gain_b[:, which, :], op0=ALU.mult, op1=ALU.mult).then_inc(xn_ready, 1)

            def add_output(p, i, n, banks):
                dve.wait_ge(wo_done, i * NT + (NT * PAIRS * p + n + 1 + CREDIT))
                t = first_tile(p) + n
                for c in range(HALVES):
                    part = h[:, t, c * BANK:(c + 1) * BANK]
                    ins = dve.tensor_tensor(part, banks[c], part, ALU.add)
                ins.then_inc(h_added, 1)

            def stick0(p, i, u):
                w = (first_tile(p) + u % NT + 1) * P
                n = STEPS * PAIRS * p + u
                dve.wait_ge(gates_ready, i * STEPS + (n + 1))
                dve.tensor_tensor_scan(left[:, u % 2, BANK - w:BANK][:, ::-1], fail[:, u % 2, 0:w][:, ::-1],
                                       fail[:, u % 2, 0:w][:, ::-1], 1.0, ALU.mult, ALU.bypass).then_inc(left_ready, 1)
                if u >= 2:
                    dve.wait_ge(attnT_done, i * STEPS + (n - 1))
                dve.wait_ge(left_ready, i * STEPS + (n + 1))
                dve.tensor_tensor(attn[:, u % 2, 0:w], take[:, u % 2, 0:w], left[:, u % 2, BANK + 1 - w:BANK + 1],
                                  ALU.mult).then_inc(attn_ready, 1)

            def head_sums1(p, i, lo):
                w = 2 * NS if lo in (0, GROUP) else NS
                dve.wait_ge(q_copied, i + (PAIRS * (p % 2) + 1))
                dve.tensor_reduce(head_ss[:, 0:w // DH], head_sq[:, 0:w].rearrange("p (n c) -> p n c", c=DH), AX_X,
                                  ALU.add).then_inc(headss_ready, 1)

            def head_norm1(p, i, lo):
                w = 2 * NS if lo in (0, GROUP) else NS
                tok = head_tok[:, 0:w].rearrange("p (n c) -> p n c", c=DH)
                n, q = w // DH, NS // DH
                dve.sem_clear(dve_step)
                dve.wait_ge(headroot_ready, i + (PAIRS * (p % 2) + 1))
                dve.reciprocal(head_rstd[:, 0:n], head_root[:, 0:n]).then_inc(dve_step, 1)
                dve.wait_ge(dve_step, 1)
                dve.tensor_tensor(tok, tok, spread(head_rstd[:, 0:n], 2, [P, n, DH]), ALU.mult).then_inc(dve_step, 1)
                dve.wait_ge(dve_step, 2)
                if n > q:
                    dve.tensor_tensor(tok[:, q:n, :], tok[:, q:n, :], spread(qk_gain[:, 1, :], 1, [P, n - q, DH]), ALU.mult)
                dve.tensor_tensor(tok[:, 0:q, :], tok[:, 0:q, :], spread(qk_gain[:, 0, :], 1, [P, q, DH]),
                                  ALU.mult).then_inc(headn_ready, 1)

            def biased1(p, i, a, lo):
                j = lo // GROUP
                hd = i + (GROUP * j + GROUP * a)
                slope, sink = neg_slope[:, bass.ds(hd, 1)], sink_b[:, bass.ds(hd, 1)]
                z = z_own[:].rearrange("p (n w) -> p n w", n=NT)
                base = 2 * PAIRS * (p % 2) + a + 1
                dve.sem_clear(dve_step)
                dve.wait_ge(swz_done, i * 2 + base)
                if p % 2 == 0:
                    dve.scalar_tensor_tensor(out=sw_score[:, a, 0, P:WIN], in0=dist[:, P:WIN], scalar=slope,
                                             in1=z[:, 0, P:WIN], op0=ALU.mult, op1=ALU.add)
                    dve.scalar_tensor_tensor(out=sw_score[:, a, 1, :], in0=dist[:], scalar=slope,
                                             in1=z[:, 1, :], op0=ALU.mult, op1=ALU.add).then_inc(swz_read, 1)
                else:
                    dve.scalar_tensor_tensor(out=sw_score[:, a, :, :], in0=spread(dist[:], 1, [P, NT, WIN]), scalar=slope,
                                             in1=z, op0=ALU.mult, op1=ALU.add).then_inc(swz_read, 1)
                dve.wait_ge(swz_read, i * 2 + base)
                dve.tensor_reduce(top[:, a, :], sw_score[:, a, :, :], AX_X, ALU.max).then_inc(dve_step, 1)
                dve.wait_ge(dve_step, 1)
                dve.tensor_scalar(neg_top[:, a, :], top[:, a, :], sink, -1.0, ALU.max, ALU.mult).then_inc(dve_step, 1)
                dve.wait_ge(dve_step, 2)
                dve.tensor_scalar(sink_arg[:, a, :], neg_top[:, a, :], sink, None, ALU.add).then_inc(negtop_ready, 1)

            def normalise1(p, i, a):
                dve.sem_clear(dve_step)
                dve.wait_ge(exp_ready, i * 2 + (2 * PAIRS * (p % 2) + a + 1))
                dve.tensor_tensor(denom[:, a, :], row_sum[:, a, :], sink_exp[:, a, :], ALU.add).then_inc(dve_step, 1)
                dve.wait_ge(dve_step, 1)
                dve.reciprocal(inv_denom[:, a, :], denom[:, a, :]).then_inc(dve_step, 1)
                dve.wait_ge(dve_step, 2)
                dve.tensor_tensor(prob[:, a, :, :], prob[:, a, :, :], spread(inv_denom[:, a, :], 2, [P, NT, WIN]),
                                  ALU.mult).then_inc(prob_ready, 1)

            def top16(values, others, top_out, idx_out, step):
                step(dve.max(top_out[:, 0:TOP8], values))
                step(dve.match_replace(others, top_out[:, 0:TOP8], values, LOWEST))
                step(dve.max(top_out[:, TOP8:TOPK], others))
                dve.max_index(idx_out[:, 0:TOP8], top_out[:, 0:TOP8], values)
                step(dve.max_index(idx_out[:, TOP8:TOPK], top_out[:, TOP8:TOPK], others))

            def choose(s, hd, t):
                dve.sem_clear(dve_step)
                count = [0]

                def step(ins):
                    count[0] += 1
                    ins.then_inc(dve_step, 1)
                    dve.wait_ge(dve_step, count[0])

                if t == 0:
                    dve.wait_ge(scores_ready, hd + (s * PEER_HEADS + 1))
                    dve.sem_inc(dve_step, 1)
                    count[0] = 1
                for half in range(2):
                    top16(scores[:, t, half, :], rest[:, half, :], half_top[:, half, :], half_idx[:, half, :], step)
                step(dve.tensor_tensor(cand[:], spread(half_top[:, 0, :], 2, [P, TOPK, TOPK]),
                                       spread(half_top[:, 1, :], 1, [P, TOPK, TOPK]), ALU.add))
                top16(cand[:].rearrange("p a b -> p (a b)"), cand_rest[:], cand_top[:], cand_idx[:], step)
                dve.tensor_scalar(neg_best[:], cand_top[:, 0:1], -1.0, None, ALU.mult).then_inc(best_ready, 1)
                dve.tensor_copy(half_idx_f[:], half_idx[:])
                dve.tensor_single_scalar(place[:, 0, :], cand_idx[:], 4, ALU.logical_shift_right)
                step(dve.tensor_single_scalar(place[:, 1, :], cand_idx[:], TOPK - 1, ALU.bitwise_and))
                step(dve.tensor_copy(place_f[:], place[:]))
                shape = [P, 2, TOPK, TOPK]
                step(dve.tensor_tensor(onehot[:], spread(place_f[:], 3, shape),
                                       slot_no[:].unsqueeze(1).unsqueeze(1).broadcast_to(shape), ALU.is_equal))
                step(dve.tensor_tensor(onehot[:], onehot[:], spread(half_idx_f[:], 2, shape), ALU.mult))
                step(dve.tensor_reduce(picked[:], onehot[:], AX_X, ALU.add))
                n = UNITS * s + t
                if not (isinstance(hd, int) and n + hd * NT < 2):
                    dve.wait_ge(v_slots_free, hd * (NT * TOPK) + ((n - 1) * TOPK + SLOTS))
                dve.scalar_tensor_tensor(out=expert[:, t, :], in0=picked[:, 0, :], scalar=float(KEYS),
                                         in1=picked[:, 1, :], op0=ALU.mult, op1=ALU.add).then_inc(expert_ready, 1)

            def products(s, hd, t, k0, k1):
                n = UNITS * s + t
                if k0 == 0:
                    dve.sem_clear(dve_step)
                    dve.tensor_copy(x_cur[:], xn[:, first_tile(s) + t, :]).then_inc(dve_step, 1)
                    dve.wait_ge(dve_step, 1)
                for k in range(k0, k1):
                    dve.wait_ge(u_landed[k % SLOTS], hd * (NT * 32) + (n * 32 + 16 * (k // SLOTS + 1)))
                    row = u_ring[:, k % SLOTS, :]
                    dve.tensor_tensor_reduce(row, row, x_cur[:], 1.0, 0.0, ALU.mult, ALU.add,
                                             hid[:, k:k + 1]).then_inc(u_slots_free, 1)

            def add_unit(s, hd, t):
                n = UNITS * s + t
                dve.wait_ge(v_slots_free, hd * (NT * TOPK) + ((n + 1) * TOPK + SLOTS))
                for c in range(HALVES):
                    part = h[:, first_tile(s) + t, c * BANK:(c + 1) * BANK]
                    ins = dve.tensor_tensor(part, acc[c][:], part, ALU.add)
                ins.then_inc(acc_added, 1)

            def coefficients(s, hd, t):
                n = UNITS * s + t
                count = [0]

                def step(ins):
                    count[0] += 1
                    ins.then_inc(dve_step, 1)
                    dve.wait_ge(dve_step, count[0])

                dve.sem_clear(dve_step)
                dve.wait_ge(u_slots_free, hd * (NT * TOPK) + ((n + 1) * TOPK + SLOTS))
                step(dve.tensor_tensor(g1[:], hid[:], hid[:], ALU.mult))
                step(dve.tensor_scalar(g2[:], g1[:], -GELU_C * GELU_A, -GELU_C, ALU.mult, ALU.add))
                dve.tensor_tensor(g3[:], g2[:], hid[:], ALU.mult).then_inc(gelu_arg_ready, 1)
                dve.wait_ge(gate_ready, hd * NT + (n + 1))
                dve.reciprocal(inv_gate[:], gate_sum[:])
                dve.wait_ge(gelu_exp_ready, hd * NT + (n + 1))
                step(dve.tensor_scalar(g1[:], gelu_exp[:], HUGE, 1.0, ALU.min, ALU.add))
                step(dve.reciprocal(g2[:], g1[:]))
                step(dve.tensor_tensor(g1[:], hid[:], g2[:], ALU.mult))
                dve.scalar_tensor_tensor(out=coef[:], in0=g1[:], scalar=inv_gate[:], in1=gate[:],
                                         op0=ALU.mult, op1=ALU.mult).then_inc(coef_ready, 1)

            dve.sem_inc(u_slots_free, SLOTS)
            dve.sem_inc(h_added, CREDIT)
            dve.memset(left[:, :, BANK:BANK + 1], 1.0).then_inc(dve_set, 1)
            dve.wait_ge(dve_set, 1)
            norm(0, 0, 0, attn_gain_landed, 16)
            with dve.Fori(0, PAIRS) as i:
                for u in range(STEPS):
                    stick0(0, i, u)
                add_output(0, i, 0, [t_own[:], acc[1][:]])
                add_output(0, i, 1, [x_cur[:, BANK:D], vo_bank[:]])
            for s in range(STAGES):
                p = s + 1
                if s == 0:
                    norm(1, 0, 1, peer_gain_landed, 16)
                    choose(0, 0, 0)
                    norm(2, 1, 0, attn_gain_landed, 16)
                if p == 2:
                    dve.wait_ge(small_landed, 48)
                    dve.memset(sw_score[:, :, 0, 0:P], MASKED).then_inc(dve_set, 1)
                    dve.memset(prob[:, :, 0, 0:P], 0.0).then_inc(dve_set, 1)
                    dve.tensor_scalar(qk_gain[:, 0, :], qk_gain[:, 0, :], SCALE, None, ALU.mult).then_inc(dve_set, 1)
                    dve.wait_ge(dve_set, 4)

                def iteration(hd, first, last, lo):
                    turn = last and p < STAGES
                    if not first:
                        choose(s, hd, 0)
                    if first and s == 0:
                        products(s, hd, 0, 0, TOPK)
                    elif first:
                        products(s, hd, 0, 0, 6)
                        add_unit(s - 1, PEER_HEADS - 1, NT - 1)
                        products(s, hd, 0, 6, 10)
                        if p < STAGES:
                            norm(2 * s + 2, p, 0, attn_gain_landed, 16 * (p // 2 + 1))
                        products(s, hd, 0, 10, TOPK)
                    else:
                        products(s, hd, 0, 0, 8)
                        add_unit(s, hd - 1, NT - 1)
                        products(s, hd, 0, 8, 10)
                        if p < STAGES:
                            add_output(p, hd - 1, 0, [z_own[:], t_own[:]])
                        products(s, hd, 0, 10, TOPK)
                    if turn and p > 1:
                        head_sums1(p, hd, lo)
                    coefficients(s, hd, 0)
                    if p < STAGES and not first:
                        add_output(p, hd - 1, 1, [qk_bank[:], vo_bank[:]])
                    if turn and p > 1:
                        head_norm1(p, hd, lo)
                    elif p in (2, 3) and not first:
                        head_sums1(p, hd, lo)
                    choose(s, hd, 1)
                    if p == 1:
                        for u in range(STEPS if turn else NT):
                            stick0(p, hd, u)
                    elif turn:
                        biased1(p, hd, 0, lo)
                        biased1(p, hd, 1, lo)
                        normalise1(p, hd, 0)
                        normalise1(p, hd, 1)
                    elif p < STAGES:
                        if first:
                            head_sums1(p, hd, lo)
                        head_norm1(p, hd, lo)
                    products(s, hd, 1, 0, 8)
                    add_unit(s, hd, 0)
                    if turn:
                        add_output(p, hd, 0, [z_own[:], t_own[:]])
                        add_output(p, hd, 1, [qk_bank[:], vo_bank[:]])
                        products(s, hd, 1, 8, 11)
                        norm(2 * p + 1, p, 1, peer_gain_landed, 16 * (p // 2 + 1))
                        products(s, hd, 1, 11, TOPK)
                    elif p in (2, 3):
                        products(s, hd, 1, 8, 13)
                        biased1(p, hd, 0, lo)
                        products(s, hd, 1, 13, TOPK)
                    else:
                        products(s, hd, 1, 8, TOPK)
                    coefficients(s, hd, 1)
                    if turn:
                        choose(p, 0, 0)
                    elif p == 1:
                        stick0(p, hd, 2)
                        stick0(p, hd, 3)
                    elif p < STAGES:
                        biased1(p, hd, 1, lo)
                        normalise1(p, hd, 0)
                        normalise1(p, hd, 1)

                run(dve, s, iteration)
            n = UNITS * STAGES - 1
            dve.wait_ge(coef_ready, n + 1)
            for k in range(LAST_ROWS, TOPK):
                dve.sem_clear(dve_step)
                dve.wait_ge(v_landed[k % SLOTS], 32 * n + 16 * (k // SLOTS + 1))
                part = h[:, TT - 1, :]
                dve.scalar_tensor_tensor(out=part, in0=v_ring[:, k % SLOTS, :], scalar=coef[:, k:k + 1], in1=part,
                                         op0=ALU.mult, op1=ALU.add).then_inc(dve_step, 1)
                dve.wait_ge(dve_step, 1)
            dve.wait_ge(v_slots_free, TOPK * n + LAST_ROWS + SLOTS)
            for c in range(HALVES):
                part = h[:, TT - 1, c * BANK:(c + 1) * BANK]
                ins = dve.tensor_tensor(part, acc[c][:], part, ALU.add)
            ins.then_inc(acc_added, 1)


_INS = ['x', 'sb_norm', 'sb_w_qkv', 'sb_w_o', 'sw_norm', 'sw_w_qkv', 'sw_q_gain', 'sw_k_gain', 'sw_sinks', 'sw_w_o',
        'ffn_norm', 'peer_w_query', 'peer_sub_keys', 'peer_u', 'peer_v']
_OUT = ((1, S, D), 'float32')


def kernel(**inputs):
    import concourse.bacc as bacc
    from concourse.bass_utils import run_bass_kernel_spmd

    nc = bacc.Bacc("TRN2", target_bir_lowering=False, num_devices=1)
    arrays, args = {}, []
    for name in _INS:
        a = np.ascontiguousarray(inputs[name])
        arrays[f"in_{name}"] = a
        args.append(nc.dram_tensor(f"in_{name}", a.shape, mybir.dt.from_np(a.dtype), kind="ExternalInput").ap())
    shape, dtype = _OUT
    args.append(nc.dram_tensor("out_h", shape, mybir.dt.from_np(np.dtype(dtype)), kind="ExternalOutput").ap())
    build(nc, *args)
    r = run_bass_kernel_spmd(nc, [arrays], core_ids=[0])
    return r.results[0]["out_h"]
```
